# Optimizing a Trainium2 kernel written in Bass

```python
import math
import jax, jax.numpy as jnp
from jax import lax
import numpy as np

D_MODEL = 1024
BATCH = 1
SEQ = 256
DEPTH = 2

N_ATTN = (DEPTH + 1) // 2
N_LRU = DEPTH // 2
N_DENSE = (DEPTH + 1) // 2
N_MOE = DEPTH // 2

N_HEADS = 8
HEAD_DIM = D_MODEL // N_HEADS // 2
V_DIM = 2 * HEAD_DIM
Q_BLOCK = 128
SCALE = HEAD_DIM ** -0.5
NEG_INF = -1e30

NUM_BUCKETS = 32
MAX_EXACT = NUM_BUCKETS // 2
MAX_DISTANCE = 128

D_RNN = 1280
N_LRU_BLOCKS = 10
LRU_BLOCK = D_RNN // N_LRU_BLOCKS
CONV_WIDTH = 4
LRU_C = 8.0

D_FF = 2816
N_EXPERTS = 8
TOP_K = 2
D_FF_EXPERT = 3584

NORM_EPS = 1e-6
SUBLN_EPS = 1e-5

kernel_name = "hybrid_diffattn_rglru_moe"

def rmsnorm(x, g, eps=NORM_EPS):
    xf = x.astype(jnp.float32)
    y = xf * lax.rsqrt(jnp.mean(xf * xf, axis=-1, keepdims=True) + eps)
    return (y * g.astype(jnp.float32)).astype(x.dtype)

def t5_bucket(n):
    nf = jnp.maximum(n, 1).astype(jnp.float32)
    large = MAX_EXACT + (jnp.log(nf / MAX_EXACT) / math.log(MAX_DISTANCE / MAX_EXACT)
                         * (NUM_BUCKETS - MAX_EXACT)).astype(jnp.int32)
    large = jnp.minimum(large, NUM_BUCKETS - 1)
    return jnp.where(n < MAX_EXACT, n, large)

def diff_attention(h, w_qkv, w_o, lq1, lk1, lq2, lk2, subln_g, rel_bias, lam_init):
    B, S, _ = h.shape
    q, k, v = jnp.split(h @ w_qkv, 3, axis=-1)
    q = q.reshape(B, S, N_HEADS, 2, HEAD_DIM)
    k = k.reshape(B, S, N_HEADS, 2, HEAD_DIM)
    v = v.reshape(B, S, N_HEADS, V_DIM)
    lam = (jnp.exp(jnp.sum(lq1.astype(jnp.float32) * lk1.astype(jnp.float32)))
           - jnp.exp(jnp.sum(lq2.astype(jnp.float32) * lk2.astype(jnp.float32)))
           + lam_init)
    nb = S // Q_BLOCK
    qb = q.reshape(B, nb, Q_BLOCK, N_HEADS, 2, HEAD_DIM).transpose(1, 0, 2, 3, 4, 5)
    k_pos = jnp.arange(S, dtype=jnp.int32)

    def block(args):
        q_blk, blk = args
        q_pos = blk * Q_BLOCK + jnp.arange(Q_BLOCK, dtype=jnp.int32)
        dist = q_pos[:, None] - k_pos[None, :]
        bias = rel_bias[t5_bucket(jnp.maximum(dist, 0))]
        bias = jnp.transpose(bias, (2, 0, 1)).astype(jnp.float32)[None, :, None]
        s = jnp.einsum('bqhcd,bkhcd->bhcqk', q_blk, k).astype(jnp.float32) * SCALE + bias
        s = jnp.where(dist >= 0, s, NEG_INF)
        p = jax.nn.softmax(s, axis=-1)
        a = p[:, :, 0] - lam * p[:, :, 1]
        return jnp.einsum('bhqk,bkhe->bqhe', a.astype(v.dtype), v)

    o = lax.map(block, (qb, jnp.arange(nb, dtype=jnp.int32)))
    o = o.transpose(1, 0, 2, 3, 4).reshape(B, S, N_HEADS, V_DIM)
    o = rmsnorm(o, subln_g, SUBLN_EPS) * (1.0 - lam_init)
    return o.reshape(B, S, N_HEADS * V_DIM) @ w_o

def _lin_combine(c1, c2):
    a1, b1 = c1
    a2, b2 = c2
    return a1 * a2, a2 * b1 + b2

def rglru_block(h, w_in, conv_w, conv_b, ga_w, ga_b, gx_w, gx_b, lam_param, w_out):
    B, S, _ = h.shape
    gate_br, x_br = jnp.split(h @ w_in, 2, axis=-1)
    gate_br = jax.nn.gelu(gate_br)
    xp = jnp.pad(x_br, ((0, 0), (CONV_WIDTH - 1, 0), (0, 0)))
    xc = conv_b + sum(xp[:, j:j + S] * conv_w[j] for j in range(CONV_WIDTH))
    xblk = xc.reshape(B, S, N_LRU_BLOCKS, LRU_BLOCK)
    r = jax.nn.sigmoid(jnp.einsum('bsnd,nde->bsne', xblk, ga_w).reshape(B, S, D_RNN) + ga_b)
    i = jax.nn.sigmoid(jnp.einsum('bsnd,nde->bsne', xblk, gx_w).reshape(B, S, D_RNN) + gx_b)
    log_a = -LRU_C * r.astype(jnp.float32) * jax.nn.softplus(-lam_param.astype(jnp.float32))
    a = jnp.exp(log_a)
    mult = jnp.sqrt(-jnp.expm1(2.0 * log_a))
    b = mult * (i * xc).astype(jnp.float32)
    _, hs = lax.associative_scan(_lin_combine, (a, b), axis=1)
    y = hs.astype(h.dtype) * gate_br
    return y @ w_out

def swiglu(t, wg, wu, wd):
    return (jax.nn.silu(t @ wg) * (t @ wu)) @ wd

def moe_swiglu(h, router, wg, wu, wd):
    B, S, D = h.shape
    t = h.reshape(B * S, D)
    logits = (t @ router).astype(jnp.float32)
    top_v, top_i = lax.top_k(logits, TOP_K)
    gates = jax.nn.softmax(top_v, axis=-1)
    comb = jnp.sum(jax.nn.one_hot(top_i, N_EXPERTS, dtype=jnp.float32) * gates[..., None], axis=1)
    out = jnp.zeros_like(t)
    for e in range(N_EXPERTS):
        out = out + comb[:, e:e + 1].astype(t.dtype) * swiglu(t, wg[e], wu[e], wd[e])
    return out.reshape(B, S, D)

def setup_inputs(seed: int = 0) -> dict:
    key = jax.random.key(seed)
    ks = iter(jax.random.split(key, 40))

    def w(shape, fan_in):
        return jax.random.normal(next(ks), shape, jnp.float32) * (fan_in ** -0.5)

    def gain(shape):
        return 1.0 + 0.01 * jax.random.normal(next(ks), shape, jnp.float32)

    def small(shape, s=0.01):
        return s * jax.random.normal(next(ks), shape, jnp.float32)

    x = jax.random.normal(next(ks), (BATCH, SEQ, D_MODEL), jnp.float32)
    u = jax.random.uniform(next(ks), (N_LRU, D_RNN), jnp.float32, 0.9, 0.999)
    a0 = u ** (1.0 / LRU_C)
    lru_lambda = jnp.log(a0) - jnp.log1p(-a0)
    return {
        "x": x,
        "norm_mix": gain((DEPTH, D_MODEL)),
        "norm_ffn": gain((DEPTH, D_MODEL)),
        "norm_final": gain((D_MODEL,)),
        "rel_bias": small((NUM_BUCKETS, N_HEADS), 0.5),
        "attn_w_qkv": w((N_ATTN, D_MODEL, 3 * D_MODEL), D_MODEL),
        "attn_w_o": w((N_ATTN, N_HEADS * V_DIM, D_MODEL), N_HEADS * V_DIM),
        "attn_lambda_q1": small((N_ATTN, HEAD_DIM), 0.1),
        "attn_lambda_k1": small((N_ATTN, HEAD_DIM), 0.1),
        "attn_lambda_q2": small((N_ATTN, HEAD_DIM), 0.1),
        "attn_lambda_k2": small((N_ATTN, HEAD_DIM), 0.1),
        "attn_subln": gain((N_ATTN, V_DIM)),
        "lru_w_in": w((N_LRU, D_MODEL, 2 * D_RNN), D_MODEL),
        "lru_conv_w": w((N_LRU, CONV_WIDTH, D_RNN), CONV_WIDTH),
        "lru_conv_b": small((N_LRU, D_RNN)),
        "lru_gate_a_w": w((N_LRU, N_LRU_BLOCKS, LRU_BLOCK, LRU_BLOCK), LRU_BLOCK),
        "lru_gate_a_b": small((N_LRU, D_RNN)),
        "lru_gate_x_w": w((N_LRU, N_LRU_BLOCKS, LRU_BLOCK, LRU_BLOCK), LRU_BLOCK),
        "lru_gate_x_b": small((N_LRU, D_RNN)),
        "lru_lambda": lru_lambda,
        "lru_w_out": w((N_LRU, D_RNN, D_MODEL), D_RNN),
        "ffn_w_gate": w((N_DENSE, D_MODEL, D_FF), D_MODEL),
        "ffn_w_up": w((N_DENSE, D_MODEL, D_FF), D_MODEL),
        "ffn_w_down": w((N_DENSE, D_FF, D_MODEL), D_FF),
        "moe_router": w((N_MOE, D_MODEL, N_EXPERTS), D_MODEL),
        "moe_w_gate": w((N_MOE, N_EXPERTS, D_MODEL, D_FF_EXPERT), D_MODEL),
        "moe_w_up": w((N_MOE, N_EXPERTS, D_MODEL, D_FF_EXPERT), D_MODEL),
        "moe_w_down": w((N_MOE, N_EXPERTS, D_FF_EXPERT, D_MODEL), D_FF_EXPERT),
    }

def reference(x, norm_mix, norm_ffn, norm_final, rel_bias,
              attn_w_qkv, attn_w_o, attn_lambda_q1, attn_lambda_k1, attn_lambda_q2, attn_lambda_k2, attn_subln,
              lru_w_in, lru_conv_w, lru_conv_b, lru_gate_a_w, lru_gate_a_b, lru_gate_x_w, lru_gate_x_b,
              lru_lambda, lru_w_out,
              ffn_w_gate, ffn_w_up, ffn_w_down,
              moe_router, moe_w_gate, moe_w_up, moe_w_down):
    for i in range(DEPTH):
        h = rmsnorm(x, norm_mix[i])
        if i % 2 == 0:
            j = i // 2
            lam_init = 0.8 - 0.6 * math.exp(-0.3 * i)
            m = diff_attention(h, attn_w_qkv[j], attn_w_o[j], attn_lambda_q1[j], attn_lambda_k1[j],
                               attn_lambda_q2[j], attn_lambda_k2[j], attn_subln[j], rel_bias, lam_init)
        else:
            j = i // 2
            m = rglru_block(h, lru_w_in[j], lru_conv_w[j], lru_conv_b[j], lru_gate_a_w[j], lru_gate_a_b[j],
                            lru_gate_x_w[j], lru_gate_x_b[j], lru_lambda[j], lru_w_out[j])
        x = x + m
        h = rmsnorm(x, norm_ffn[i])
        if i % 2 == 0:
            j = i // 2
            f = swiglu(h, ffn_w_gate[j], ffn_w_up[j], ffn_w_down[j])
        else:
            j = i // 2
            f = moe_swiglu(h, moe_router[j], moe_w_gate[j], moe_w_up[j], moe_w_down[j])
        x = x + f
    return rmsnorm(x, norm_final)


_drawn_inputs = setup_inputs


def setup_inputs(seed=0):
    import zlib

    import numpy as np

    out = dict(_drawn_inputs(seed))
    spreads = {}
    factors = {'norm_ffn': 3.116,
     'norm_final': 191.026,
     'attn_lambda_k1': 3.835,
     'attn_lambda_q2': 3.912,
     'attn_subln': 3.074,
     'lru_gate_a_b': 29.649,
     'lru_gate_x_b': 52.992,
     'lru_conv_b': 8.0}
    for name, (base, spread) in spreads.items():
        noise = np.random.default_rng([zlib.crc32(name.encode()), seed]).standard_normal(out[name].shape)
        drawn = base * np.exp(spread * noise) if base else spread * noise
        out[name] = __import__('jax').numpy.asarray(drawn.astype(out[name].dtype))
    for name, factor in factors.items():
        out[name] = (out[name] * factor).astype(out[name].dtype)
    return out
```

```python
import math
from contextlib import ExitStack

import numpy as np

import concourse.bass as bass
from concourse import mybir

F32 = mybir.dt.float32
F32R = mybir.dt.float32r
BF16 = mybir.dt.bfloat16
I32 = mybir.dt.int32
ALU = mybir.AluOpType
ACT = mybir.ActivationFunctionType
AX_X = mybir.AxisListType.X

P = 128


def bucket_of(n, buckets, max_exact, max_distance):
    if n < max_exact:
        return n
    f = np.float32
    large = f(np.log(f(n) / f(max_exact))) / f(math.log(max_distance / max_exact)) * f(buckets - max_exact)
    return min(max_exact + int(large), buckets - 1)


def build_trunk(nc, x, norm_mix, norm_ffn, norm_final, rel_bias, w_qkv, w_o, lq1, lk1, lq2, lk2, subln,
                w_in, conv_w, conv_b, ga_w, ga_b, gx_w, gx_b, lam_p, w_out,
                f_gate, f_up, f_down, router, m_gate, m_up, m_down, out):
    _, S, D = x.shape
    NB = S // P
    KC = D // P
    HEADS = rel_bias.shape[1]
    BUCKETS = rel_bias.shape[0]
    HD = lq1.shape[1]
    VD = 2 * HD
    SCALE = HD ** -0.5
    LAM_INIT = 0.8 - 0.6 * math.exp(0.0)
    R = w_out.shape[1]
    RB = R // P
    FF = f_gate.shape[2]
    E = m_gate.shape[1]
    FE = m_gate.shape[3]
    CW = 512
    EC = FE // CW
    FC = FF // CW
    XP = 3
    NEG = -1e30
    assert (S, D, VD, FE % CW, FF - FC * CW, RB % 2) == (256, 1024, P, 0, 256, 0)
    assert P + (2 * S - 1) // P <= P + XP and (XP + 1) * (P + 1) > 2 * S

    PIECE = 2048

    def cols4(w, half, c0):
        return w.rearrange("(c p) n -> p c n", p=P)[:, 4 * half:4 * half + 4, c0:c0 + 512]

    def cols8(w, c0):
        return w.rearrange("(c p) n -> p c n", p=P)[:, :, c0:c0 + 256]

    def rows2(w, r0):
        return w[r0:r0 + 256, :].rearrange("(s p) n -> p s n", p=P)

    static = []
    wq = w_qkv[0]
    for part in range(2):
        for pair in range(2):
            static += [cols8(wq, 512 * part + 256 * pair), cols8(wq, D + 512 * part + 256 * pair)]
        static += [cols4(wq, h, 2 * D + 512 * part) for h in range(2)]
    P_WO = len(static)
    static += [cols4(w_o[0], h, 512 * g) for h in range(2) for g in range(2)]
    P_FFN = len(static)
    fg, fu, fd = f_gate[0], f_up[0], f_down[0]
    for i in range(FC):
        static += [cols4(fg, h, CW * i) for h in range(2)]
        if i:
            static += [rows2(fd, CW * (i - 1) + 256 * h) for h in range(2)]
        static += [cols4(fu, h, CW * i) for h in range(2)]
    static += [cols8(fg, CW * FC)] + [rows2(fd, CW * (FC - 1) + 256 * h) for h in range(2)]
    static += [cols8(fu, CW * FC), rows2(fd, CW * FC)]

    def f_gate_at(i):
        return P_FFN + (0 if i == 0 else 6 * i - 2)

    def f_up_at(i):
        return P_FFN + 2 if i == 0 else f_gate_at(i) + (4 if i < FC else 3)

    def f_down_at(i):
        return f_gate_at(i + 1) + (2 if i + 1 < FC else 1) if i < FC else f_up_at(FC) + 1
    P_IN = len(static)
    static += [cols8(w_in[0], R + 256 * j) for j in range(RB // 2)]
    static += [cols8(w_in[0], 256 * j) for j in range(RB // 2)]
    P_OUT = len(static)
    static += [rows2(w_out[0], 256 * j) for j in range(RB // 2)]
    P_MOE = len(static)
    PASS = EC * 6

    XR, WR, HR = 3, 4, 4
    assert PASS % (XR + WR) == 0 and P_MOE % WR == 0
    HALF = [s for size in (4, 4, 4, 3, 4, 4, 4, 4, 3, 4, 4) for s in range(size)]
    assert len(HALF) == PASS

    def land_slot(n):
        return XR + n % WR if n < P_MOE else (n - P_MOE) % (XR + WR)

    def land_back(n):
        return WR if n < P_MOE else XR + WR

    def landings(n):
        return sum(land_slot(m) == land_slot(n) for m in range(n + 1))

    LANDINGS = PASS // (XR + WR)

    def half_slot(n):
        return HALF[(n - P_MOE) % PASS]

    def half_back(n):
        return next(d for d in range(1, PASS) if half_slot(n - d) == half_slot(n))

    mg = m_gate.rearrange("a e (c p) f -> (a e) p c f", p=P)
    mu = m_up.rearrange("a e (c p) f -> (a e) p c f", p=P)
    md = m_down.rearrange("a e (s p) n -> (a e) p s n", p=P)

    def expert_pieces(e):
        pieces = []
        for i in range(EC):
            pieces += [mg[e, :, 4 * h:4 * h + 4, CW * i:CW * i + CW] for h in range(2)]
            pieces += [mu[e, :, 4 * h:4 * h + 4, CW * i:CW * i + CW] for h in range(2)]
            if i:
                pieces += [md[e, :, 4 * (i - 1) + 2 * h:4 * (i - 1) + 2 * h + 2, :] for h in range(2)]
        pieces += [md[e, :, 4 * (EC - 1) + 2 * h:4 * (EC - 1) + 2 * h + 2, :] for h in range(2)]
        return pieces

    def at(i):
        return 0 if i == 0 else 4 + 6 * (i - 1)

    rel_scratch = nc.dram_tensor("rel_scratch", [HEADS, 3 * P], F32).ap()

    with ExitStack() as ctx:
        def sb(name, shape, dt=F32):
            return ctx.enter_context(nc.sbuf_tensor(name, shape, dt))

        def sem(name):
            return ctx.enter_context(nc.semaphore(name))

        w_ring = sb("w_ring", [P, WR, PIECE])
        w_hi = sb("w_hi", [P, HR, PIECE], F32R)
        w_lo = sb("w_lo", [P, HR, PIECE], F32R)
        xres = sb("xres", [P, NB, D])
        hn = sb("hn", [P, NB, D])
        gain = sb("gain", [P, D])
        xt_hi = sb("xt_hi", [P, KC, S], F32R)
        xt_lo = sb("xt_lo", [P, KC, S], F32R)
        split = sb("split", [P, 7680], F32R)
        work = sb("work", [P, 10760])
        ident = sb("ident", [P, P])
        iota_s = sb("iota_s", [P, P])
        tri = sb("tri", [P, P], BF16)
        ones = sb("ones", [P, P], BF16)
        rw = sb("rw", [P, KC, E])
        small = sb("small", [P, 360])
        neg_lam = small[:, 0:1]
        ss = small[:, 2:4]
        rstd = small[:, 4:6]
        nt = small[:, 6:8]
        lam_e = small[:, 10:12]
        ntmp = small[:, 12:14]
        sd = small[:, 8:10]
        prm = small[:, 16:96]
        cvw = prm[:, 0:4 * RB].rearrange("p (j n) -> p j n", j=4)
        cvb = prm[:, 4 * RB:5 * RB]
        gab = prm[:, 5 * RB:6 * RB]
        gxb = prm[:, 6 * RB:7 * RB]
        lamp = prm[:, 7 * RB:8 * RB]
        decay = small[:, 96:96 + RB]
        lt = small[:, 110:110 + 5 * RB].rearrange("p (k n) -> p k n", k=5)
        mx = small[:, 160:168].rearrange("p (h k) -> p h k", h=2)
        es = small[:, 168:176].rearrange("p (h k) -> p h k", h=2)
        er = small[:, 176:184].rearrange("p (h k) -> p h k", h=2)
        oss = small[:, 184:248].rearrange("p (k n) -> p k n", k=4)
        g_cur = small[:, 248:250]
        c_cur = small[:, 250:252]
        slots = small[:, 252:252 + NB * (E + XP + 1)].rearrange("p (b n) -> p b n", b=NB)
        combs = small[:, 276:276 + NB * (E + XP + 2)].rearrange("p (b n) -> p b n", b=NB)
        passes = small[0:1, 310:311]
        extra = small[0:1, 312:312 + XP]
        iota_e = small[:, 320:328]
        counts = small[:, 328:336]
        ranks = small[:, 336:344]
        pick = small[:, 344:352]

        qT = work[:, 0:2048].rearrange("p (h t) -> p h t", h=HEADS)
        kT = work[:, 2048:4096].rearrange("p (h t) -> p h t", h=HEADS)
        v = work[:, 4096:6144].rearrange("p (b n) -> p b n", b=NB)
        bias = work[:, 6144:8192].rearrange("p (h t) -> p h t", h=HEADS)
        ex = work[:, 8192:9728].rearrange("p (h c n) -> p h c n", h=2, c=2)
        aT = work[:, 9728:10496].rearrange("p (h n) -> p h n", h=2)
        subln_b = work[:, 10496:10624]
        lamv = work[:, 9728:9984].rearrange("p (k n) -> p k n", k=4)
        rows_in = work[:, 9984:10112]
        rel_in = work[:, 10112:10120]
        relT = work[0:HEADS, 10120:10152]
        lamj = work[:, 10152:10216]
        o_sq = gain[:, :].rearrange("p (b h e) -> p b h e", b=NB, h=4)
        rel_row = work[0:HEADS, 8192:8192 + 3 * P]
        flip = work[:, 10240:10368]
        bias_up = work[:, 4096:6144]
        act_f = work[:, 0:1024].rearrange("p (b n) -> p b n", b=NB)
        aT_hi = split[:, 0:1024].rearrange("p (s t) -> p s t", s=4)
        aT_lo = split[:, 1024:2048].rearrange("p (s t) -> p s t", s=4)
        rt = work[:, 0:2560].rearrange("p (n t) -> p n t", n=RB)
        ix = work[:, 2560:5120].rearrange("p (n t) -> p n t", n=RB)
        gate = work[:, 5120:7680].rearrange("p (n t) -> p n t", n=RB)
        wga = work[:, 7680:8960].rearrange("p (n e) -> p n e", n=RB)
        wgx = work[:, 8960:10240].rearrange("p (n e) -> p n e", n=RB)
        hs = work[:, 7680:10240].rearrange("p (n t) -> p n t", n=RB)
        xb = work[:, 10240:10240 + 2 * 259].rearrange("p (n t) -> p n t", n=2)
        xc = hn[:, 0, :].rearrange("p (j n t) -> p j n t", j=2, n=2)
        rg = hn[:, 1, 0:512].rearrange("p (n t) -> p n t", n=2)
        ig = hn[:, 1, 512:1024].rearrange("p (n t) -> p n t", n=2)
        qq = hn[:, :, :].rearrange("p b n -> p (b n)")[:, 0:1280].rearrange("p (n t) -> p n t", n=RB // 2)
        yT_hi = split[:, 0:2560].rearrange("p (n t) -> p n t", n=RB)
        yT_lo = split[:, 2560:5120].rearrange("p (n t) -> p n t", n=RB)
        act_e = work[:, 0:512]
        xtf = work[:, 704:2752].rearrange("p (c t) -> p c t", c=KC)
        rt_b = [work[:, 512 + 16 * k:528 + 16 * k].rearrange("p (b e) -> p b e", b=NB) for k in range(12)]
        h_hi = split[:, 0:2048].rearrange("p (b n) -> p b n", b=NB)
        h_lo = split[:, 2048:4096].rearrange("p (b n) -> p b n", b=NB)
        y_hi = split[:, 4096:5120]
        y_lo = split[:, 5120:6144]
        onehot = split[:, 6144:6400].rearrange("p (b s) -> p b s", b=NB)
        onehotT = split[:, 6400:6656]
        eT_hi = [split[:, 6656:7168].rearrange("p (s t) -> p s t", s=4), xt_hi[:, 0:4, P:2 * P]]
        eT_lo = [split[:, 7168:7680].rearrange("p (s t) -> p s t", s=4), xt_lo[:, 0:4, P:2 * P]]
        x_ring = work[:, 4616:4616 + XR * PIECE].rearrange("p (k n) -> p k n", k=XR)

        def land(n):
            s = land_slot(n)
            return x_ring[:, s, :] if s < XR else w_ring[:, s - XR, :]

        sel16 = sb("sel16", [P, NB, E], BF16)

        ps = ctx.enter_context(nc.psum_tensor("ps", [P, 8, 512], F32))
        GB, UB, TB, SB_, M0, M1, D0, D1 = range(8)

        landed = [sem(f"landed{s}") for s in range(XR + WR)]
        hi_ready, lo_ready, piece_used = sem("hi_ready"), sem("lo_ready"), sem("piece_used")
        in_x, in_small, in_gain, in_lru, in_rel, rel_out = (sem("in_x"), sem("in_small"), sem("in_gain"),
                                                            sem("in_lru"), sem("in_rel"), sem("rel_out"))
        consts, late_consts = sem("consts"), sem("late_consts")
        dve_link, act_link, pool_link = sem("dve_link"), sem("act_link"), sem("pool_link")
        x_ready, sq_ready, var_ready, root_ready, hn_ready = (sem("x_ready"), sem("sq_ready"), sem("var_ready"),
                                                              sem("root_ready"), sem("hn_ready"))
        xt_ps, xt_hi_ok, xt_lo_ok = sem("xt_ps"), sem("xt_hi_ok"), sem("xt_lo_ok")
        prm_ps, prm_ok, rel_ps, rel_row_ok = sem("prm_ps"), sem("prm_ok"), sem("rel_ps"), sem("rel_row_ok")
        flip_ps, bias_ok = sem("flip_ps"), sem("bias_ok")
        lam_dot, lam_exp, decay_exp, decay_in = sem("lam_dot"), sem("lam_exp"), sem("decay_exp"), sem("decay_in")
        q_out, k_out, v_out_a, v_out_d = sem("q_out"), sem("k_out"), sem("v_out_a"), sem("v_out_d")
        s_done, masked, exp_done, probs = sem("s_done"), sem("masked"), sem("exp_done"), sem("probs")
        t_done, aT_ok, o_done, o_out = sem("t_done"), sem("aT_ok"), sem("o_done"), sem("o_out")
        ovar, oroot, on_ready = sem("ovar"), sem("oroot"), sem("on_ready")
        fs, fa, ft, fh, fl = sem("f_silu"), sem("f_act"), sem("f_tr"), sem("f_hi"), sem("f_lo")
        xb_zero, gexp_in, gexp_ok = sem("xb_zero"), sem("gexp_in"), sem("gexp_ok")
        cur_ok = sem("cur_ok")
        xb_ok, xc_ok, ri_ps, ri_ok, ix_ok = sem("xb_ok"), sem("xc_ok"), sem("ri_ps"), sem("ri_ok"), sem("ix_ok")
        t_ok, sqt_ok, gelu_ok, y_ok, yh_ok, yl_ok = (sem("t_ok"), sem("sqt_ok"), sem("gelu_ok"), sem("y_ok"),
                                                     sem("yh_ok"), sem("yl_ok"))
        xtf_a, xtf_d, log_ps, sel_ok, pos_ps, route_ok = (sem("xtf_a"), sem("xtf_d"), sem("log_ps"), sem("sel_ok"),
                                                          sem("pos_ps"), sem("route_ok"))
        dl_ok, de_ok, h_hi_ok, h_lo_ok = sem("dl_ok"), sem("de_ok"), sem("h_hi_ok"), sem("h_lo_ok")
        oh_ok, oht_ps, oht_ok = sem("oh_ok"), sem("oht_ps"), sem("oht_ok")
        gat_ps, gat_hi, gat_lo = sem("gat_ps"), sem("gat_hi"), sem("gat_lo")
        es_ok, ea_ok, et_ps, eh_ok, el_ok = sem("es_ok"), sem("ea_ok"), sem("et_ps"), sem("eh_ok"), sem("el_ok")
        ys_hi, ys_lo, sc_ps, sc_ok, out_done = sem("ys_hi"), sem("ys_lo"), sem("sc_ps"), sem("sc_ok"), sem("out_done")

        block = ctx.enter_context(nc.Block())

        @block.sync
        def _(sp):
            sp.dma_start(xres[:, :, :], x[0].rearrange("(b p) n -> p b n", p=P)).then_inc(in_x, 16)
            sp.dma_start(gain[:, :], norm_mix[0:1, :].to_broadcast([P, D])).then_inc(in_gain, 16)

            def load(n, src, uses=0):
                if n >= WR:
                    sp.wait_ge(lo_ready, uses * PASS + (n - land_back(n) + 1))
                dst = land(n)[:, 0:src.shape[1] * src.shape[2]]
                sp.dma_start(dst.rearrange("p (c n) -> p c n", c=src.shape[1]), src).then_inc(landed[land_slot(n)], 16)

            for n in range(WR):
                load(n, static[n])
            sp.wait_ge(rel_row_ok, 1)
            sp.dma_start(rel_scratch, rel_row).then_inc(rel_out, 16)
            sp.wait_ge(rel_out, 16)
            skew = bass.AP(rel_scratch.tensor, 0, [[1, P], [3 * P, HEADS], [1, S]])
            sp.dma_start(bias_up, skew).then_inc(in_rel, 16)
            for n in range(WR, P_MOE):
                if n == P_FFN + 3:
                    sp.wait_ge(on_ready, 2)
                    sp.dma_start(gain[:, :], norm_ffn[0:1, :].to_broadcast([P, D])).then_inc(in_gain, 16)
                if n == P_IN - 3:
                    sp.wait_ge(hn_ready, 4)
                    sp.dma_start(gain[:, :], norm_mix[1:2, :].to_broadcast([P, D])).then_inc(in_gain, 16)
                    sp.dma_start(wga, ga_w[0].rearrange("n d e -> d n e")).then_inc(in_lru, 16)
                    sp.dma_start(wgx, gx_w[0].rearrange("n d e -> d n e")).then_inc(in_lru, 16)
                if n == P_OUT:
                    sp.wait_ge(hn_ready, 6)
                    sp.dma_start(gain[:, :], norm_ffn[1:2, :].to_broadcast([P, D])).then_inc(in_gain, 16)
                load(n, static[n])

            sp.wait_ge(yl_ok, RB // 2)
            with nc.sync.Fori(0, E) as p:
                for j, src in enumerate(expert_pieces(p)):
                    load(P_MOE + j, src, uses=p)
            sp.wait_ge(hn_ready, 8)
            sp.dma_start(gain[:, :], norm_final.rearrange("(a n) -> a n", a=1).to_broadcast([P, D])).then_inc(in_gain, 16)
            sp.wait_ge(route_ok, 1)
            total = nc.sync.value_load(passes.bitcast(I32), min_val=E, max_val=E + XP)
            with nc.sync.If(total > E):
                with nc.sync.Fori(E, total) as p:
                    e = nc.sync.value_load(small[0:1, bass.ds(p + (312 - E), 1)].bitcast(I32), min_val=0,
                                           max_val=E - 1)
                    for j, src in enumerate(expert_pieces(e)):
                        load(P_MOE + j, src, uses=p)
            for b in range(NB):
                sp.wait_ge(hn_ready, 9 + b)
                sp.dma_start(out[0, b * P:(b + 1) * P, :], hn[:, b, :]).then_inc(out_done, 16)
            sp.wait_ge(out_done, 16 * NB)

        @block.gpsimd
        def _(pool):
            nc.gpsimd.memset(ident[:, :], 0.0).then_inc(pool_link, 1)
            nc.gpsimd.memset(tri[:, :], 0.0).then_inc(pool_link, 1)
            nc.gpsimd.memset(flip, 0.0).then_inc(pool_link, 1)
            pool.wait_ge(pool_link, 3)
            nc.gpsimd.affine_select(out=ident[:, :], in_=ident[:, :], compare_op=ALU.not_equal, fill=1.0,
                                    base=0, pattern=[[-1, P]], channel_multiplier=1).then_inc(consts, 1)
            nc.gpsimd.affine_select(out=flip, in_=flip, compare_op=ALU.not_equal, fill=1.0,
                                    base=1 - P, pattern=[[1, P]], channel_multiplier=1).then_inc(consts, 1)
            nc.gpsimd.affine_select(out=tri[:, :], in_=tri[:, :], compare_op=ALU.is_ge, fill=1.0,
                                    base=0, pattern=[[-1, P]], channel_multiplier=1).then_inc(late_consts, 1)
            nc.gpsimd.memset(ones[:, :], 1.0).then_inc(late_consts, 1)
            nc.gpsimd.iota(iota_s[:, :], pattern=[[1, P]], base=0, channel_multiplier=0,
                           allow_small_or_imprecise_dtypes=True).then_inc(late_consts, 1)
            nc.gpsimd.iota(iota_e, pattern=[[1, E]], base=0, channel_multiplier=0,
                           allow_small_or_imprecise_dtypes=True).then_inc(late_consts, 1)

        @block.scalar
        def _(act):
            links = [0]
            done = [0]

            def copy(out, in_):
                return nc.scalar.activation(out, in_, ACT.Copy)

            def hi_upto(n):
                while done[0] <= min(n, P_MOE - 1):
                    k = done[0]
                    act.wait_ge(landed[land_slot(k)], 16 * landings(k))
                    if k >= half_back(k):
                        act.wait_ge(piece_used, k - half_back(k) + 1)
                    copy(w_hi[:, half_slot(k), :], land(k)).then_inc(hi_ready, 1)
                    done[0] += 1

            def square_sums(t):
                if t:
                    act.wait_ge(x_ready, t)
                else:
                    act.wait_ge(in_x, 16)
                for b in range(NB):
                    nc.scalar.activation(hn[:, b, :], xres[:, b, :], ACT.Square,
                                         accum_out=ss[:, b:b + 1]).then_inc(sq_ready, 1)

            def root(t):
                act.wait_ge(var_ready, t + 1)
                nc.scalar.activation(sd, nt, ACT.Sqrt).then_inc(root_ready, 1)

            def xt_split(count, banks, c0):
                for j, b in enumerate(banks):
                    act.wait_ge(xt_ps, count + j + 1)
                    copy(xt_hi[:, c0 + 2 * j:c0 + 2 * j + 2, :],
                         ps[:, b, :].rearrange("p (c t) -> p c t", c=2)).then_inc(xt_hi_ok, 1)

            def exps(h):
                act.wait_ge(masked, 4 * (h + 1))
                for c in range(2):
                    for b in range(2):
                        seg = ex[:, h % 2, c, 256 * (1 - b):256 + 128 * (1 - b)]
                        k = 2 * c + b
                        nc.scalar.activation(seg, seg, ACT.Exp, bias=mx[:, h % 2, k:k + 1], scale=-1.0,
                                             accum_out=es[:, h % 2, k:k + 1]).then_inc(exp_done, 1)

            def aT_out(h):
                act.wait_ge(t_done, h + 1)
                if h >= 2:
                    act.wait_ge(o_done, h - 1)
                copy(aT[:, h % 2, :], ps[:, 2, 0:384]).then_inc(aT_ok, 1)

            def o_evac(h):
                act.wait_ge(o_done, h + 1)
                copy(hn[:, :, P * h:P * h + P],
                     ps[:, 3, 0:256].rearrange("p (b n) -> p b n", b=NB)).then_inc(o_out, 1)

            def q_evac(n, k):
                act.wait_ge(piece_used, n + 1)
                copy(qT[:, 2 * k:2 * k + 2, :], ps[:, 0, :].rearrange("p (h t) -> p h t", h=2)).then_inc(q_out, 1)

            def v_evac(n, part):
                act.wait_ge(piece_used, n + 1)
                copy(v[:, 0, 512 * part:512 * part + 512], ps[:, 0, :]).then_inc(v_out_a, 1)

            def head_root(k):
                act.wait_ge(ovar, k + 1)
                nc.scalar.activation(oss[:, 1, 8 * k:8 * k + 8], oss[:, 0, 8 * k:8 * k + 8],
                                     ACT.Sqrt).then_inc(oroot, 1)

            with nc.allow_non_contiguous_dma(reason="small parameters"):
                rows = [(conv_w[0, j].rearrange("(n p) -> n p", p=P), RB) for j in range(4)]
                rows += [(a[0].rearrange("(n p) -> n p", p=P), RB) for a in (conv_b, ga_b, gx_b, lam_p)]
                for k, (src, n) in enumerate(rows):
                    act.dma_start(rows_in[k * RB:k * RB + n, :], src).then_inc(in_small, 16)
                act.dma_start(rel_in[0:BUCKETS, :], rel_bias).then_inc(in_small, 16)
                for k, a in enumerate((lq1, lk1, lq2, lk2)):
                    act.dma_start(lamv[:, k, :], a[0:1, :].to_broadcast([P, HD])).then_inc(in_small, 16)
                act.dma_start(subln_b, subln[0:1, :].to_broadcast([P, VD])).then_inc(in_small, 16)
                act.dma_start(rw[:, :, :], router[0].rearrange("(c p) e -> p c e", p=P)).then_inc(in_small, 16)
            square_sums(0)
            root(0)
            act.wait_ge(lam_dot, 2)
            nc.scalar.activation(lam_e, lam_e, ACT.Exp).then_inc(lam_exp, 1)
            hi_upto(2)
            xt_split(0, range(4), 0)
            q_evac(0, 0)
            hi_upto(4)
            q_evac(2, 1)
            hi_upto(7)
            v_evac(5, 0)
            exps(0)
            hi_upto(8)
            q_evac(6, 2)
            hi_upto(9)
            aT_out(0)
            exps(1)
            hi_upto(10)
            o_evac(0)
            exps(2)
            aT_out(1)
            hi_upto(11)
            q_evac(8, 3)
            o_evac(1)
            aT_out(2)
            exps(3)
            hi_upto(12)
            o_evac(2)
            aT_out(3)
            hi_upto(14)
            v_evac(11, 1)
            o_evac(3)
            exps(4)
            head_root(0)
            xt_split(4, (6, 7), 0)
            aT_out(4)
            exps(5)
            o_evac(4)
            hi_upto(15)
            aT_out(5)
            exps(6)
            o_evac(5)
            aT_out(6)
            exps(7)
            o_evac(6)
            aT_out(7)
            o_evac(7)
            hi_upto(16)
            head_root(1)
            xt_split(6, (2, 3), 4)
            act.wait_ge(dl_ok, 1)
            nc.scalar.activation(lt[:, 1, :], lt[:, 0, :], ACT.Exp, scale=-1.0).then_inc(de_ok, 1)
            hi_upto(P_FFN + 2)
            square_sums(1)
            root(1)
            xt_split(8, range(4), 0)

            def aT_split_hi(k, subs):
                act.wait_ge(ft, k + 1)
                b = k % 2
                copy(aT_hi[:, 0:subs, P * b:P * b + P],
                     ps[:, 2 + b, 0:P * subs].rearrange("p (s t) -> p s t", s=subs)).then_inc(fh, 1)

            for i in range(FC + 1):
                last = i == FC
                hi_upto(f_gate_at(i) + 2)
                if i:
                    aT_split_hi(2 * i - 2, 4)
                    aT_split_hi(2 * i - 1, 4)
                hi_upto(f_gate_at(i) + (2 if last else 3))
                act.wait_ge(piece_used, f_gate_at(i) + (1 if last else 2))
                for b in range(NB):
                    cols = 256 if last else CW
                    nc.scalar.activation(act_f[:, b, 0:cols], ps[:, b, 0:cols], ACT.Silu).then_inc(fs, 1)
            hi_upto(P_IN + 1)
            aT_split_hi(2 * FC, 2)
            aT_split_hi(2 * FC + 1, 2)

            hi_upto(P_IN + 2)
            square_sums(2)
            root(2)
            xt_split(12, range(4), 0)
            for j in range(RB // 2):
                act.wait_ge(piece_used, P_IN + j + 1)
                if j:
                    act.wait_ge(xc_ok, j)
                else:
                    act.wait_ge(xb_zero, 1)
                copy(xb[:, :, 3:3 + S], ps[:, j % 2, :].rearrange("p (n t) -> p n t", n=2)).then_inc(xb_ok, 1)
                hi_upto(P_IN + j + 3)
                act.wait_ge(ri_ps, j + 1)
                if j:
                    act.wait_ge(ix_ok, j)
                for m in range(2):
                    b = 2 * j + m
                    nc.scalar.activation(ig[:, m, :], ps[:, 3, 256 * m:256 * m + 256], ACT.Sigmoid,
                                         bias=gxb[:, b:b + 1]).then_inc(ri_ok, 1)
                    nc.scalar.activation(rg[:, m, :], ps[:, 2, 256 * m:256 * m + 256], ACT.Sigmoid,
                                         bias=gab[:, b:b + 1]).then_inc(act_link, 1)
                    links[0] += 1
                act.wait_ge(act_link, links[0])
                for m in range(2):
                    b = 2 * j + m
                    nc.scalar.activation(rt[:, b, :], rg[:, m, :], ACT.Tanh,
                                         scale=decay[:, b:b + 1]).then_inc(t_ok, 1)
            act.wait_ge(t_ok, RB)
            nc.scalar.activation(hs, rt, ACT.Sqrt, scale=-1.0).then_inc(sqt_ok, 1)
            for j in range(RB // 2):
                act.wait_ge(piece_used, P_IN + RB // 2 + j + 1)
                nc.scalar.activation(gate[:, 2 * j:2 * j + 2, :], ps[:, 6 + j % 2, :].rearrange("p (n t) -> p n t", n=2),
                                     ACT.Gelu_apprx_tanh).then_inc(gelu_ok, 1)
                hi_upto(P_IN + RB // 2 + j + 3)
            for j in range(RB // 2):
                act.wait_ge(y_ok, j + 1)
                copy(yT_hi[:, 2 * j:2 * j + 2, :], gate[:, 2 * j:2 * j + 2, :]).then_inc(yh_ok, 1)
                hi_upto(P_OUT + j + 2)

            hi_upto(P_MOE - 1)
            square_sums(3)
            root(3)
            for j in range(0, 4, 2):
                act.wait_ge(xt_ps, 16 + j + 1)
                copy(xtf[:, 2 * j:2 * j + 2, :], ps[:, j, :].rearrange("p (c t) -> p c t", c=2)).then_inc(xtf_a, 1)
            act.wait_ge(hn_ready, 8)
            act.wait_ge(piece_used, P_MOE)
            for b in range(NB):
                copy(h_hi[:, b, :], hn[:, b, :]).then_inc(h_hi_ok, 1)
            act.wait_ge(gexp_in, 1)
            nc.scalar.activation(rt_b[8][:, :, 1:2], rt_b[8][:, :, 0:1], ACT.Exp).then_inc(gexp_ok, 1)

            def gathered_hi(count):
                for j, b in enumerate((M0, M1)):
                    act.wait_ge(gat_ps, count + j + 1)
                    copy(xt_hi[:, 4 * j:4 * j + 4, 0:P], ps[:, b, :].rearrange("p (c t) -> p c t", c=4)).then_inc(gat_hi, 1)

            gathered_hi(0)
            act.wait_ge(route_ok, 1)
            total = nc.scalar.value_load(passes.bitcast(I32), min_val=E, max_val=E + XP)
            nc.scalar.sem_inc(es_ok, 1)
            with nc.scalar.Fori(0, total) as p:
                def hi(j):
                    n = P_MOE + j
                    act.wait_ge(landed[land_slot(n)], p * (16 * LANDINGS) + 16 * landings(n))
                    act.wait_ge(piece_used, p * PASS + (n - half_back(n) + 1))
                    copy(w_hi[:, half_slot(n), :], land(n)).then_inc(hi_ready, 1)

                def eT_split_hi(i):
                    act.wait_ge(et_ps, p * EC + (i + 2))
                    copy(eT_hi[i % 2], ps[:, TB, :].rearrange("p (s t) -> p s t", s=4)).then_inc(eh_ok, 1)

                def silu(i):
                    act.wait_ge(piece_used, p * PASS + (P_MOE + at(i) + 2))
                    act.wait_ge(et_ps, p * EC + (i + 1))
                    nc.scalar.activation(act_e, ps[:, GB, :], ACT.Silu).then_inc(es_ok, 1)

                hi(0)
                hi(1)
                act.wait_ge(piece_used, p * PASS + P_MOE)
                copy(y_hi, ps[:, D0:D0 + 2, :].rearrange("p a n -> p (a n)")).then_inc(ys_hi, 1)
                hi(2)
                hi(3)
                hi(4)
                silu(0)
                for i in range(1, EC):
                    g0 = at(i)
                    for j in range(0 if i > 1 else 1, 6):
                        hi(g0 + j)
                    eT_split_hi(i - 1)
                    silu(i)
                hi(PASS - 2)
                hi(PASS - 1)
                for j, b in enumerate((M0, M1)):
                    act.wait_ge(gat_ps, p * 4 + (4 + j + 1))
                    copy(xt_hi[:, 4 * j:4 * j + 4, 0:P],
                         ps[:, b, :].rearrange("p (c t) -> p c t", c=4)).then_inc(gat_hi, 1)
                eT_split_hi(EC - 1)
            act.wait_ge(piece_used, total * PASS + P_MOE)
            copy(y_hi, ps[:, D0:D0 + 2, :].rearrange("p a n -> p (a n)")).then_inc(ys_hi, 1)
            act.wait_ge(sc_ok, total * 4 + 4)
            for b in range(NB):
                nc.scalar.activation(hn[:, b, :], xres[:, b, :], ACT.Square, accum_out=ss[:, b:b + 1]).then_inc(sq_ready, 1)
            root(4)

        @block.vector
        def _(dve):
            links = [0]
            done = [0]
            V = nc.vector

            def link(ins):
                links[0] += 1
                ins.then_inc(dve_link, 1)
                dve.wait_ge(dve_link, links[0])

            def lo_upto(n):
                while done[0] <= min(n, P_MOE - 1):
                    k = done[0]
                    dve.wait_ge(hi_ready, k + 1)
                    V.tensor_tensor(w_lo[:, half_slot(k), :], land(k), w_hi[:, half_slot(k), :].bitcast(F32),
                                    ALU.subtract).then_inc(lo_ready, 1)
                    done[0] += 1

            def rsqrt(out, var, root_of, tmp, step=link):
                step(V.reciprocal(out, root_of))
                step(V.tensor_tensor(tmp, out, out, ALU.mult))
                step(V.tensor_tensor(tmp, tmp, var, ALU.mult))
                step(V.tensor_scalar(tmp, tmp, -0.5, 1.5, ALU.mult, ALU.add))
                step(V.tensor_tensor(out, out, tmp, ALU.mult))

            def norm(t):
                dve.wait_ge(sq_ready, 2 * t + 2)
                link(V.tensor_scalar(nt, ss, 1.0 / D, 1e-6, ALU.mult, ALU.add))
                V.tensor_copy(ntmp, nt).then_inc(var_ready, 1)
                dve.wait_ge(root_ready, t + 1)
                rsqrt(rstd, nt, sd, ntmp)
                dve.wait_ge(in_gain, 16 * (t + 1))
                for b in range(NB):
                    V.scalar_tensor_tensor(hn[:, b, :], xres[:, b, :], rstd[:, b:b + 1], gain[:, :],
                                           ALU.mult, ALU.mult).then_inc(hn_ready, 1)

            def xt_split(count, banks, c0):
                for j, b in enumerate(banks):
                    dve.wait_ge(xt_hi_ok, count + j + 1)
                    V.tensor_tensor(xt_lo[:, c0 + 2 * j:c0 + 2 * j + 2, :], ps[:, b, :].rearrange("p (c t) -> p c t", c=2),
                                    xt_hi[:, c0 + 2 * j:c0 + 2 * j + 2, :].bitcast(F32),
                                    ALU.subtract).then_inc(xt_lo_ok, 1)

            def mask(h):
                dve.wait_ge(s_done, h + 1)
                if h == 0:
                    dve.wait_ge(bias_ok, 1)
                if h >= 2:
                    dve.wait_ge(t_done, h - 1)
                for c in range(2):
                    for b in range(2):
                        n0, n1 = 256 * (1 - b), 256 + 128 * (1 - b)
                        k = 2 * c + b
                        V.tensor_tensor_reduce(out=ex[:, h % 2, c, n0:n1], in0=ps[:, 4 + c, n0:n1],
                                               in1=bias[:, h, P * (1 - b):S], scale=-SCALE, scalar=3e38, op0=ALU.add,
                                               op1=ALU.min, accum_out=mx[:, h % 2, k:k + 1]).then_inc(masked, 1)

            def mix(h):
                dve.wait_ge(exp_done, 4 * (h + 1))
                r, e = er[:, h % 2], ex[:, h % 2]
                link(V.reciprocal(r, es[:, h % 2]))
                link(V.tensor_scalar(r[:, 2:4], r[:, 2:4], neg_lam, None, ALU.mult))
                V.tensor_scalar(e[:, 0, 0:256], e[:, 0, 0:256], r[:, 1:2], None, ALU.mult)
                link(V.tensor_scalar(e[:, 0, 256:384], e[:, 0, 256:384], r[:, 0:1], None, ALU.mult))
                V.scalar_tensor_tensor(e[:, 0, 0:256], e[:, 1, 0:256], r[:, 3:4], e[:, 0, 0:256], ALU.mult, ALU.add)
                V.scalar_tensor_tensor(e[:, 0, 256:384], e[:, 1, 256:384], r[:, 2:3], e[:, 0, 256:384],
                                       ALU.mult, ALU.add).then_inc(probs, 1)

            def k_evac(n, k):
                dve.wait_ge(piece_used, n + 1)
                V.tensor_copy(kT[:, 2 * k:2 * k + 2, :], ps[:, 1, :].rearrange("p (h t) -> p h t", h=2)).then_inc(k_out, 1)

            def v_evac(n, part):
                dve.wait_ge(piece_used, n + 1)
                V.tensor_copy(v[:, 1, 512 * part:512 * part + 512], ps[:, 1, :]).then_inc(v_out_d, 1)

            def head_norm(k):
                dve.wait_ge(o_out, 4 * k + 4)
                o = hn[:, :, 512 * k:512 * k + 512].rearrange("p b (h e) -> p b h e", h=4)

                def st(i):
                    return oss[:, i, 8 * k:8 * k + 8]
                link(V.tensor_tensor(o_sq, o, o, ALU.mult))
                link(V.tensor_reduce(st(2).rearrange("p (b h) -> p b h", b=NB), o_sq, axis=AX_X, op=ALU.add))
                V.tensor_scalar(st(0), st(2), 1.0 / VD, 1e-5, ALU.mult, ALU.add).then_inc(ovar, 1)
                dve.wait_ge(oroot, k + 1)
                rsqrt(st(2), st(0), st(1), st(3))
                for b in range(NB):
                    link(V.tensor_tensor(o[:, b], o[:, b],
                                         st(2)[:, 4 * b:4 * b + 4].unsqueeze(2).to_broadcast([P, 4, VD]), ALU.mult))
                for b in range(NB):
                    ins = V.tensor_tensor(o[:, b], o[:, b], subln_b.unsqueeze(1).to_broadcast([P, 4, VD]), ALU.mult)
                ins.then_inc(on_ready, 1)

            def add_to_x(banks):
                for k, bank in enumerate(banks):
                    b, half = divmod(k, 2)
                    xs = xres[:, b, 512 * half:512 * half + 512]
                    ins = V.tensor_tensor(xs, xs, ps[:, bank, :], ALU.add)
                    if k == 3:
                        ins.then_inc(x_ready, 1)

            dve.wait_ge(rel_ps, 1)
            link(V.tensor_scalar(relT, ps[0:HEADS, 6, 0:BUCKETS], 1.0 / SCALE, None, ALU.mult))
            buckets = [bucket_of(n, BUCKETS, BUCKETS // 2, 128) for n in range(S)]
            V.memset(rel_row[:, S:3 * P], NEG / SCALE)
            for k in range(BUCKETS):
                n0, n1 = buckets.index(k), S - buckets[::-1].index(k)
                ins = V.tensor_copy(rel_row[:, S - n1:S - n0], relT[:, k:k + 1].to_broadcast([HEADS, n1 - n0]))
            ins.then_inc(rel_row_ok, 1)
            dve.wait_ge(in_small, 16 * 15)
            for k in range(2):
                V.tensor_tensor_reduce(out=lamj, in0=lamv[:, 2 * k, :], in1=lamv[:, 2 * k + 1, :], scale=1.0, scalar=0.0,
                                       op0=ALU.mult, op1=ALU.add, accum_out=lam_e[:, k:k + 1]).then_inc(lam_dot, 1)
                dve.wait_ge(lam_dot, k + 1)
            V.tensor_scalar(subln_b, subln_b, 1.0 - LAM_INIT, None, ALU.mult).then_inc(dve_link, 1)
            links[0] += 1
            norm(0)
            lo_upto(0)
            xt_split(0, range(4), 0)
            lo_upto(2)
            dve.wait_ge(prm_ps, 1)
            V.tensor_copy(prm, ps[:, 7, 0:8 * RB]).then_inc(prm_ok, 1)
            dve.wait_ge(lam_exp, 1)
            V.scalar_tensor_tensor(neg_lam, lam_e[:, 1:2], -LAM_INIT, lam_e[:, 0:1], ALU.add,
                                   ALU.subtract).then_inc(dve_link, 1)
            links[0] += 1
            lo_upto(3)
            k_evac(1, 0)
            lo_upto(5)
            k_evac(3, 1)
            dve.wait_ge(flip_ps, 1)
            V.tensor_copy(bias, ps[:, 4:8, :].rearrange("p a (h t) -> p (a h) t", h=2)).then_inc(bias_ok, 1)
            lo_upto(7)
            v_evac(5, 0)
            mask(0)
            lo_upto(8)
            mix(0)
            lo_upto(9)
            mask(1)
            k_evac(7, 2)
            lo_upto(10)
            mix(1)
            mask(2)
            lo_upto(11)
            mix(2)
            k_evac(9, 3)
            mask(3)
            lo_upto(12)
            mix(3)
            lo_upto(14)
            v_evac(11, 1)
            mask(4)
            head_norm(0)
            mix(4)
            xt_split(4, (6, 7), 0)
            mask(5)
            mix(5)
            mask(6)
            mix(6)
            lo_upto(15)
            mask(7)
            mix(7)
            lo_upto(16)
            head_norm(1)
            xt_split(6, (2, 3), 4)
            dve.wait_ge(prm_ok, 1)
            link(V.tensor_scalar(lt[:, 0, :], lamp, -1.0, None, ALU.mult))
            V.tensor_tensor(lt[:, 0, :], lt[:, 0, :], lamp, ALU.max).then_inc(dl_ok, 1)
            dve.wait_ge(de_ok, 1)
            link(V.tensor_scalar(lt[:, 2, :], lt[:, 1, :], 2.0, None, ALU.add))
            link(V.reciprocal(lt[:, 2, :], lt[:, 2, :]))
            link(V.tensor_tensor(lt[:, 1, :], lt[:, 1, :], lt[:, 2, :], ALU.mult))
            link(V.tensor_tensor(lt[:, 2, :], lt[:, 1, :], lt[:, 1, :], ALU.mult))
            link(V.tensor_scalar(lt[:, 3, :], lt[:, 2, :], 1.0 / 17, None, ALU.mult))
            for k in range(15, 1, -2):
                link(V.scalar_tensor_tensor(lt[:, 3, :], lt[:, 3, :], 1.0 / k, lt[:, 2, :], ALU.add, ALU.mult))
            link(V.scalar_tensor_tensor(lt[:, 3, :], lt[:, 3, :], 1.0, lt[:, 1, :], ALU.add, ALU.mult))
            link(V.tensor_scalar(lt[:, 4, :], lamp, -1.0, 0.0, ALU.mult, ALU.max))
            link(V.scalar_tensor_tensor(lt[:, 4, :], lt[:, 3, :], 2.0, lt[:, 4, :], ALU.mult, ALU.add))
            V.tensor_scalar(decay, lt[:, 4, :], -4.0, None, ALU.mult).then_inc(decay_in, 1)
            dve.wait_ge(piece_used, P_FFN)
            add_to_x((6, 7, 0, 1))
            lo_upto(P_FFN + 2)
            norm(1)
            xt_split(8, range(4), 0)

            def aT_split_lo(k, subs):
                dve.wait_ge(fh, k + 1)
                b = k % 2
                V.tensor_tensor(aT_lo[:, 0:subs, P * b:P * b + P],
                                ps[:, 2 + b, 0:P * subs].rearrange("p (s t) -> p s t", s=subs),
                                aT_hi[:, 0:subs, P * b:P * b + P].bitcast(F32), ALU.subtract).then_inc(fl, 1)

            for i in range(FC + 1):
                last = i == FC
                lo_upto(f_gate_at(i) + 2)
                if i:
                    aT_split_lo(2 * i - 2, 4)
                    aT_split_lo(2 * i - 1, 4)
                up_end = f_up_at(i) + (1 if last else 2)
                lo_upto(up_end + 1)
                dve.wait_ge(piece_used, up_end)
                for b in range(NB):
                    cols = 256 if last else CW
                    dve.wait_ge(fs, 2 * i + b + 1)
                    V.tensor_tensor(act_f[:, b, 0:cols], act_f[:, b, 0:cols], ps[:, 2 + b, 0:cols],
                                    ALU.mult).then_inc(fa, 1)
            aT_split_lo(2 * FC, 2)
            aT_split_lo(2 * FC + 1, 2)
            lo_upto(P_IN + 2)
            dve.wait_ge(piece_used, P_IN)
            add_to_x((4, 5, 6, 7))

            norm(2)
            V.memset(xb[:, :, 0:3], 0.0).then_inc(xb_zero, 1)
            xt_split(12, range(4), 0)

            def times(j):
                dve.wait_ge(ri_ok, 2 * j + 2)
                V.tensor_tensor(ix[:, 2 * j:2 * j + 2, :], ig, xc[:, j % 2], ALU.mult).then_inc(ix_ok, 1)

            for j in range(RB // 2):
                lo_upto(P_IN + j + 2)
                dve.wait_ge(xb_ok, j + 1)
                if j >= 2:
                    dve.wait_ge(ri_ps, j - 1)
                for m in range(2):
                    b = 2 * j + m
                    V.tensor_scalar(xc[:, j % 2, m, :], xb[:, m, 3:3 + S], cvw[:, 3, b:b + 1], cvb[:, b:b + 1],
                                    ALU.mult, ALU.add).then_inc(dve_link, 1)
                links[0] += 2
                dve.wait_ge(dve_link, links[0])
                for tap in range(3):
                    for m in range(2):
                        b = 2 * j + m
                        ins = V.scalar_tensor_tensor(xc[:, j % 2, m, :], xb[:, m, tap:tap + S], cvw[:, tap, b:b + 1],
                                                     xc[:, j % 2, m, :], ALU.mult, ALU.add)
                        if (tap, m) == (2, 1):
                            ins.then_inc(xc_ok, 1)
                        else:
                            ins.then_inc(dve_link, 1)
                            links[0] += 1
                    if tap < 2:
                        dve.wait_ge(dve_link, links[0])
                if j:
                    times(j - 1)
            lo_upto(P_IN + RB // 2 + 2)
            dve.wait_ge(xc_ok, RB // 2)
            times(RB // 2 - 1)
            dve.wait_ge(t_ok, RB)
            dve.wait_ge(ix_ok, RB // 2)
            for g in range(2):
                n0, n1 = g * RB // 2, (g + 1) * RB // 2
                link(V.tensor_scalar(qq, rt[:, n0:n1, :], -1.0, 1.0, ALU.mult, ALU.add))
                link(V.reciprocal(qq, qq))
                dve.wait_ge(sqt_ok, 1)
                link(V.scalar_tensor_tensor(hs[:, n0:n1, :], hs[:, n0:n1, :], 2.0, qq, ALU.mult, ALU.mult))
                link(V.scalar_tensor_tensor(rt[:, n0:n1, :], rt[:, n0:n1, :], 1.0, qq, ALU.add, ALU.mult))
                lo_upto(P_IN + RB // 2 + 3 + g)
                link(V.tensor_tensor(ix[:, n0:n1, :], ix[:, n0:n1, :], hs[:, n0:n1, :], ALU.mult))
                for n in range(n0, n1):
                    V.tensor_tensor_scan(hs[:, n, :], rt[:, n, :], ix[:, n, :], 0.0, ALU.mult,
                                         ALU.add).then_inc(dve_link, 1)
                    links[0] += 1
                lo_upto(P_IN + RB // 2 + 5 + g)
            dve.wait_ge(dve_link, links[0])
            for j in range(RB // 2):
                pair = gate[:, 2 * j:2 * j + 2, :]
                dve.wait_ge(gelu_ok, j + 1)
                V.tensor_tensor(pair, pair, hs[:, 2 * j:2 * j + 2, :], ALU.mult).then_inc(y_ok, 1)
                dve.wait_ge(yh_ok, j + 1)
                V.tensor_tensor(yT_lo[:, 2 * j:2 * j + 2, :], pair, yT_hi[:, 2 * j:2 * j + 2, :].bitcast(F32),
                                ALU.subtract).then_inc(yl_ok, 1)
                lo_upto(P_OUT + j + 2)
            lo_upto(P_MOE - 1)
            dve.wait_ge(piece_used, P_MOE)
            add_to_x((2, 3, 4, 5))

            norm(3)
            dve.wait_ge(late_consts, 4)
            V.memset(onehotT.bitcast(F32), 0.0).then_inc(oht_ok, 1)
            V.memset(combs[:, :, 0:1], 0.0)
            V.memset(slots[:, :, E + XP:E + XP + 1], -1.0)
            V.memset(rt_b[9], 1.0)
            for j in range(1, 4, 2):
                dve.wait_ge(xt_ps, 16 + j + 1)
                V.tensor_copy(xtf[:, 2 * j:2 * j + 2, :], ps[:, j, :].rearrange("p (c t) -> p c t", c=2)).then_inc(xtf_d, 1)
            for b in range(NB):
                dve.wait_ge(h_hi_ok, b + 1)
                V.tensor_tensor(h_lo[:, b, :], hn[:, b, :], h_hi[:, b, :].bitcast(F32), ALU.subtract).then_inc(h_lo_ok, 1)

            def bc(a):
                return a.to_broadcast([P, NB, E])

            def over_blocks(a):
                return a.unsqueeze(1).to_broadcast([P, NB, E])

            lg, eq, oh1, oh2, comb, sel, tmp = rt_b[0], rt_b[1], rt_b[2], rt_b[3], rt_b[4], rt_b[5], rt_b[6]
            m1, m2, mi = rt_b[7][:, :, 0:1], rt_b[7][:, :, 1:2], rt_b[7][:, :, 2:3]
            diff, e2, g1, g2 = (rt_b[8][:, :, k:k + 1] for k in range(4))
            order = rt_b[10][:, 0, :]
            dve.wait_ge(log_ps, 1)
            V.tensor_scalar(order, iota_e, -1.0, float(E), ALU.mult, ALU.add)
            link(V.tensor_copy(lg, ps[:, M0, 0:NB * E].rearrange("p (b e) -> p b e", b=NB)))

            def top(src, m, oh):
                link(V.tensor_reduce(m, src, axis=AX_X, op=ALU.max))
                link(V.tensor_tensor(eq, src, bc(m), ALU.is_equal))
                link(V.tensor_tensor(eq, eq, over_blocks(order), ALU.mult))
                link(V.tensor_reduce(mi, eq, axis=AX_X, op=ALU.max))
                link(V.tensor_tensor(oh, eq, bc(mi), ALU.is_equal))

            top(lg, m1, oh1)
            link(V.scalar_tensor_tensor(lg, oh1, -3e38, lg, ALU.mult, ALU.add))
            top(lg, m2, oh2)
            V.tensor_tensor(diff, m2, m1, ALU.subtract).then_inc(gexp_in, 1)
            link(V.tensor_tensor(sel, oh1, oh2, ALU.add))
            V.tensor_copy(sel16[:, :, :], sel).then_inc(sel_ok, 1)
            dve.wait_ge(gexp_ok, 1)
            link(V.tensor_scalar(g1, e2, 1.0, None, ALU.add))
            link(V.reciprocal(g1, g1))
            link(V.tensor_tensor(g2, e2, g1, ALU.mult))
            link(V.tensor_tensor(oh1, oh1, bc(g1), ALU.mult))
            link(V.tensor_tensor(oh2, oh2, bc(g2), ALU.mult))
            link(V.tensor_tensor(comb, oh1, oh2, ALU.add))
            V.tensor_copy(combs[:, :, 1:1 + E], comb)
            dve.wait_ge(pos_ps, 1)
            link(V.scalar_tensor_tensor(tmp, ps[:, M1, 0:NB * E].rearrange("p (b e) -> p b e", b=NB), 1.0, sel,
                                        ALU.add, ALU.mult))
            link(V.tensor_scalar(slots[:, :, 0:E], tmp, -1.0, None, ALU.add))

            def build_onehot(col, step):
                step(V.tensor_copy(g_cur.unsqueeze(2), col))
                for b in range(NB):
                    V.tensor_scalar(onehot[:, b, :], iota_s[:, :], g_cur[:, b:b + 1], None,
                                    ALU.is_equal).then_inc(oh_ok, 1)

            build_onehot(slots[:, :, 0:1], link)
            link(V.tensor_scalar(counts, ps[:, M1, NB * E:(NB + 1) * E], float(P), None, ALU.is_gt))
            link(V.tensor_tensor_scan(ranks, rt_b[9][:, 0, :], counts, 0.0, ALU.mult, ALU.add))
            V.tensor_scalar(passes.bitcast(I32), ranks[0:1, E - 1:E], float(E), None, ALU.add)
            for k in range(XP):
                link(V.scalar_tensor_tensor(pick, ranks, float(k + 1), counts, ALU.is_equal, ALU.mult))
                link(V.tensor_tensor(tmp, slots[:, :, 0:E], over_blocks(pick), ALU.mult))
                link(V.tensor_reduce(mi, tmp, axis=AX_X, op=ALU.add))
                V.tensor_scalar(slots[:, :, E + k:E + k + 1], mi, float(-P), None, ALU.add)
                link(V.tensor_tensor(tmp, comb, over_blocks(pick), ALU.mult))
                V.tensor_reduce(combs[:, :, E + k + 1:E + k + 2], tmp, axis=AX_X, op=ALU.add)
                link(V.tensor_tensor(pick, pick, iota_e, ALU.mult))
                link(V.tensor_reduce(m1[:, 0, :], pick, axis=AX_X, op=ALU.add))
                link(V.tensor_copy(extra[:, k:k + 1].bitcast(I32), m1[0:1, 0, :]))
            link(V.memset(pick, 0.0))
            V.memset(pick, 0.0).then_inc(route_ok, 1)

            for j, b in enumerate((GB, SB_)):
                dve.wait_ge(gat_ps, 2 + j + 1)
                V.tensor_copy(xt_lo[:, 4 * j:4 * j + 4, 0:P],
                              ps[:, b, :].rearrange("p (c t) -> p c t", c=4)).then_inc(gat_lo, 1)

            dve.wait_ge(route_ok, 1)
            total = V.value_load(passes.bitcast(I32), min_val=E, max_val=E + XP)
            V.sem_inc(ea_ok, 1)
            V.sem_inc(el_ok, 1)
            with V.Fori(0, total) as p:
                def lo(j):
                    n = P_MOE + j
                    dve.wait_ge(hi_ready, p * PASS + (n + 1))
                    V.tensor_tensor(w_lo[:, half_slot(n), :], land(n), w_hi[:, half_slot(n), :].bitcast(F32),
                                    ALU.subtract).then_inc(lo_ready, 1)

                def eT_split_lo(i):
                    dve.wait_ge(eh_ok, p * EC + (i + 1))
                    V.tensor_tensor(eT_lo[i % 2], ps[:, TB, :].rearrange("p (s t) -> p s t", s=4),
                                    eT_hi[i % 2].bitcast(F32), ALU.subtract).then_inc(el_ok, 1)

                def gated(i):
                    dve.wait_ge(piece_used, p * PASS + (P_MOE + at(i) + 4))
                    dve.wait_ge(es_ok, p * EC + (i + 2))
                    V.tensor_tensor(act_e, act_e, ps[:, UB, :], ALU.mult).then_inc(ea_ok, 1)

                lo(0)
                lo(1)
                dve.wait_ge(ys_hi, p + 1)
                V.tensor_tensor(y_lo, ps[:, D0:D0 + 2, :].rearrange("p a n -> p (a n)"), y_hi.bitcast(F32),
                                ALU.subtract).then_inc(ys_lo, 1)
                V.tensor_copy(c_cur.unsqueeze(2), combs[:, :, bass.ds(p, 1)]).then_inc(cur_ok, 1)
                lo(2)
                lo(3)
                dve.wait_ge(cur_ok, p * 2 + 1)
                for k, bank in enumerate((M0, M1, SB_, TB)):
                    b, half = divmod(k, 2)
                    xs = xres[:, b, 512 * half:512 * half + 512]
                    dve.wait_ge(sc_ps, p * 4 + (k + 1))
                    V.scalar_tensor_tensor(xs, ps[:, bank, :], c_cur[:, b:b + 1], xs, ALU.mult,
                                           ALU.add).then_inc(sc_ok, 1)
                lo(4)
                gated(0)
                for i in range(1, EC):
                    g0 = at(i)
                    for j in range(1, 6):
                        lo(g0 + j)
                    eT_split_lo(i - 1)
                    if i == 1:
                        dve.wait_ge(oht_ps, p + 1)
                        V.tensor_copy(onehotT, ps[:, SB_, 0:S]).then_inc(oht_ok, 1)
                    if i == 3:
                        dve.wait_ge(oht_ps, p + 1)
                        V.tensor_copy(g_cur.unsqueeze(2), slots[:, :, bass.ds(p + 1, 1)]).then_inc(cur_ok, 1)
                        dve.wait_ge(cur_ok, p * 2 + 2)
                        for b in range(NB):
                            V.tensor_scalar(onehot[:, b, :], iota_s[:, :], g_cur[:, b:b + 1], None,
                                            ALU.is_equal).then_inc(oh_ok, 1)
                    lo(g0 + 6)
                    gated(i)
                lo(PASS - 1)
                for j, b in enumerate((GB, SB_)):
                    dve.wait_ge(gat_ps, p * 4 + (4 + 2 + j + 1))
                    V.tensor_copy(xt_lo[:, 4 * j:4 * j + 4, 0:P],
                                  ps[:, b, :].rearrange("p (c t) -> p c t", c=4)).then_inc(gat_lo, 1)
                eT_split_lo(EC - 1)
            dve.wait_ge(ys_hi, total + 1)
            V.tensor_tensor(y_lo, ps[:, D0:D0 + 2, :].rearrange("p a n -> p (a n)"), y_hi.bitcast(F32),
                            ALU.subtract).then_inc(ys_lo, 1)
            V.tensor_copy(c_cur.unsqueeze(2), combs[:, :, bass.ds(total, 1)]).then_inc(cur_ok, 1)
            dve.wait_ge(cur_ok, total * 2 + 1)
            for k, bank in enumerate((M0, M1, SB_, TB)):
                b, half = divmod(k, 2)
                xs = xres[:, b, 512 * half:512 * half + 512]
                dve.wait_ge(sc_ps, total * 4 + (k + 1))
                V.scalar_tensor_tensor(xs, ps[:, bank, :], c_cur[:, b:b + 1], xs, ALU.mult, ALU.add).then_inc(sc_ok, 1)
            norm(4)

        @block.tensor
        def _(pe):
            T = nc.tensor

            def mm3(acc, xh, xl, wh, wl, start, stop, weights_stay=False):
                terms = ((xh, wh), (xl, wh), (xh, wl))
                for k, (a, b) in enumerate(terms):
                    stationary, moving = (b, a) if weights_stay else (a, b)
                    ins = T.matmul(acc, stationary, moving, start=start and k == 0, stop=stop and k == 2)
                return ins

            def piece(n):
                pe.wait_ge(lo_ready, n + 1)
                return w_hi[:, half_slot(n), :], w_lo[:, half_slot(n), :]

            def project8(n, bank):
                wh, wl = (w.rearrange("p (c n) -> p c n", c=KC) for w in piece(n))
                for m in range(2):
                    for c in range(KC):
                        ins = mm3(ps[:, bank, 256 * m:256 * m + 256], xt_hi[:, c, :], xt_lo[:, c, :],
                                  wh[:, c, P * m:P * m + P], wl[:, c, P * m:P * m + P], c == 0, c == KC - 1, True)
                ins.then_inc(piece_used, 1)

            def project4(n, banks, half, c_of=0, close=None):
                wh, wl = (w.rearrange("p (c n) -> p c n", c=4) for w in piece(n))
                for c in range(4):
                    for b, bank in enumerate(banks):
                        t = slice(P * b, P * b + P)
                        ins = mm3(ps[:, bank, :], xt_hi[:, 4 * half + c, t], xt_lo[:, 4 * half + c, t],
                                  wh[:, c, :], wl[:, c, :], half == 0 and c == 0, half == 1 and c == 3)
                ins.then_inc(piece_used, 1)

            def down(n, banks, ah, al, subs, first, last):
                wh, wl = (w.rearrange("p (s n) -> p s n", s=2) for w in piece(n))
                for s, sub in enumerate(subs):
                    for k, bank in enumerate(banks):
                        b, half = divmod(k, 2)
                        t, o = slice(P * b, P * b + P), slice(512 * half, 512 * half + 512)
                        ins = mm3(ps[:, bank, :], ah[:, sub, t], al[:, sub, t], wh[:, s, o], wl[:, s, o],
                                  first and s == 0, last and s == 1)
                ins.then_inc(piece_used, 1)

            def transpose_hn(banks, c0):
                for j, bank in enumerate(banks):
                    for m in range(2):
                        c = c0 + 2 * j + m
                        for b in range(NB):
                            o = 256 * m + P * b
                            ins = T.transpose(ps[:, bank, o:o + P], hn[:, b, P * c:P * c + P], ident[:, :])
                    ins.then_inc(xt_ps, 1)

            def scores(h):
                if h:
                    pe.wait_ge(masked, 4 * h)
                pe.wait_ge(q_out, h // 2 + 1)
                pe.wait_ge(k_out, h // 2 + 1)
                for c in range(2):
                    rows = slice(HD * c, HD * c + HD)
                    T.matmul(ps[:, 4 + c, 0:256], qT[rows, h, P:S], kT[rows, h, 0:S], start=True, stop=True)
                    ins = T.matmul(ps[:, 4 + c, 256:384], qT[rows, h, 0:P], kT[rows, h, 0:P], start=True, stop=True)
                ins.then_inc(s_done, 1)

            def turn(h):
                pe.wait_ge(probs, h + 1)
                if h:
                    pe.wait_ge(aT_ok, h)
                for k in range(3):
                    ins = T.transpose(ps[:, 2, P * k:P * k + P], ex[:, h % 2, 0, P * k:P * k + P], ident[:, :])
                ins.then_inc(t_done, 1)

            def values(h):
                pe.wait_ge(aT_ok, h + 1)
                pe.wait_ge(v_out_a, h // 4 + 1)
                pe.wait_ge(v_out_d, h // 4 + 1)
                if h:
                    pe.wait_ge(o_out, h)
                e = slice(VD * h, VD * h + VD)
                a = aT[:, h % 2, :]
                T.matmul(ps[:, 3, 0:P], a[:, 256:384], v[:, 0, e], start=True, stop=True)
                T.matmul(ps[:, 3, P:2 * P], a[:, 0:128], v[:, 0, e], start=True, stop=False)
                T.matmul(ps[:, 3, P:2 * P], a[:, 128:256], v[:, 1, e], start=False, stop=True).then_inc(o_done, 1)

            pe.wait_ge(consts, 2)
            pe.wait_ge(in_small, 16 * 15)
            T.transpose(ps[0:HEADS, 6, 0:BUCKETS], rel_in[0:BUCKETS, :], ident[0:BUCKETS, 0:BUCKETS]).then_inc(rel_ps, 1)
            T.transpose(ps[:, 7, 0:8 * RB], rows_in[0:8 * RB, :], ident[0:8 * RB, 0:8 * RB]).then_inc(prm_ps, 1)
            pe.wait_ge(hn_ready, 2)
            transpose_hn(range(4), 0)
            pe.wait_ge(xt_lo_ok, 4)
            project8(0, 0)
            project8(1, 1)
            pe.wait_ge(q_out, 1)
            project8(2, 0)
            pe.wait_ge(k_out, 1)
            project8(3, 1)
            pe.wait_ge(in_rel, 16)
            pe.wait_ge(prm_ok, 1)
            for k in range(4):
                ins = T.matmul(ps[:, 4 + k, :], flip, bias_up[:, 512 * k:512 * k + 512], start=True, stop=True)
            ins.then_inc(flip_ps, 1)
            pe.wait_ge(q_out, 2)
            pe.wait_ge(k_out, 2)
            project4(4, (0, 1), 0)
            project4(5, (0, 1), 1)
            pe.wait_ge(bias_ok, 1)
            scores(0)
            pe.wait_ge(v_out_a, 1)
            project8(6, 0)
            scores(1)
            turn(0)
            pe.wait_ge(v_out_d, 1)
            project8(7, 1)
            scores(2)
            values(0)
            turn(1)
            pe.wait_ge(q_out, 3)
            project8(8, 0)
            scores(3)
            values(1)
            turn(2)
            pe.wait_ge(k_out, 3)
            project8(9, 1)
            values(2)
            turn(3)
            pe.wait_ge(q_out, 4)
            pe.wait_ge(k_out, 4)
            project4(10, (0, 1), 0)
            project4(11, (0, 1), 1)
            values(3)
            scores(4)
            pe.wait_ge(on_ready, 1)
            transpose_hn((6, 7), 0)
            turn(4)
            scores(5)
            pe.wait_ge(xt_lo_ok, 6)
            pe.wait_ge(v_out_a, 2)
            pe.wait_ge(v_out_d, 2)

            def attn_out(n, half, g):
                project4(n, ((6, 0), (7, 1))[g], half)

            attn_out(P_WO, 0, 0)
            values(4)
            turn(5)
            scores(6)
            attn_out(P_WO + 1, 0, 1)
            values(5)
            turn(6)
            scores(7)
            values(6)
            turn(7)
            values(7)
            pe.wait_ge(on_ready, 2)
            pe.wait_ge(aT_ok, 8)
            pe.wait_ge(o_out, 8)
            transpose_hn((2, 3), 4)
            pe.wait_ge(xt_lo_ok, 8)
            attn_out(P_WO + 2, 1, 0)
            attn_out(P_WO + 3, 1, 1)

            pe.wait_ge(hn_ready, 4)
            transpose_hn(range(4), 0)
            pe.wait_ge(xt_lo_ok, 12)

            def turn_chunk(i, subs):
                for b in range(NB):
                    pe.wait_ge(fa, 2 * i + b + 1)
                    for s in range(subs):
                        ins = T.transpose(ps[:, 2 + b, P * s:P * s + P], act_f[:, b, P * s:P * s + P], ident[:, :])
                    ins.then_inc(ft, 1)

            def narrow(n, banks):
                wh, wl = (w.rearrange("p (c n) -> p c n", c=KC) for w in piece(n))
                for c in range(KC):
                    for b, bank in enumerate(banks):
                        t = slice(P * b, P * b + P)
                        ins = mm3(ps[:, bank, 0:256], xt_hi[:, c, t], xt_lo[:, c, t], wh[:, c, :], wl[:, c, :],
                                  c == 0, c == KC - 1)
                ins.then_inc(piece_used, 1)

            for i in range(FC + 1):
                last = i == FC
                if i:
                    pe.wait_ge(fs, 2 * i)
                if last:
                    narrow(f_gate_at(i), (0, 1))
                    turn_chunk(i - 1, 4)
                else:
                    project4(f_gate_at(i), (0, 1), 0)
                    if i:
                        turn_chunk(i - 1, 4)
                    project4(f_gate_at(i) + 1, (0, 1), 1)
                if i:
                    pe.wait_ge(fl, 2 * i)
                    for h in range(2):
                        down(f_down_at(i - 1) + h, (4, 5, 6, 7), aT_hi, aT_lo, (2 * h, 2 * h + 1), i == 1 and h == 0, False)
                if last:
                    narrow(f_up_at(i), (2, 3))
                else:
                    project4(f_up_at(i), (2, 3), 0)
                    project4(f_up_at(i) + 1, (2, 3), 1)
            turn_chunk(FC, 2)
            pe.wait_ge(fl, 2 * FC + 2)
            down(f_down_at(FC), (4, 5, 6, 7), aT_hi, aT_lo, (0, 1), False, True)

            pe.wait_ge(hn_ready, 6)
            transpose_hn(range(4), 0)
            pe.wait_ge(xt_lo_ok, 16)
            pe.wait_ge(in_lru, 32)

            def gates(j):
                pe.wait_ge(xc_ok, j + 1)
                if j:
                    pe.wait_ge(t_ok, 2 * j)
                for m in range(2):
                    for w, bank in ((wga, 2), (wgx, 3)):
                        ins = T.matmul(ps[:, bank, 256 * m:256 * m + 256], w[:, 2 * j + m, :], xc[:, j % 2, m, :],
                                       start=True, stop=True)
                ins.then_inc(ri_ps, 1)

            for j in range(RB // 2):
                if j >= 2:
                    pe.wait_ge(xb_ok, j - 1)
                project8(P_IN + j, j % 2)
                if j:
                    gates(j - 1)
            for j in range(RB // 2):
                if j >= 2:
                    pe.wait_ge(gelu_ok, j - 1)
                project8(P_IN + RB // 2 + j, 6 + j % 2)
                if j == 0:
                    gates(RB // 2 - 1)
            pe.wait_ge(t_ok, RB)
            for j in range(RB // 2):
                pe.wait_ge(yl_ok, j + 1)
                down(P_OUT + j, (2, 3, 4, 5), yT_hi, yT_lo, (2 * j, 2 * j + 1), j == 0, j == RB // 2 - 1)

            pe.wait_ge(hn_ready, 8)
            transpose_hn(range(4), 0)
            pe.wait_ge(xtf_a, 2)
            pe.wait_ge(xtf_d, 2)
            for b in range(NB):
                for c in range(KC):
                    ins = T.matmul(ps[:, M0, E * b:E * b + E], xtf[:, c, P * b:P * b + P], rw[:, c, :],
                                   start=c == 0, stop=c == KC - 1)
            ins.then_inc(log_ps, 1)
            pe.wait_ge(late_consts, 4)
            pe.wait_ge(sel_ok, 1)
            T.matmul(ps[:, M1, 0:E], tri[:, :], sel16[:, 0, :], start=True, stop=True)
            T.matmul(ps[:, M1, E:2 * E], ones[:, :], sel16[:, 0, :], start=True, stop=False)
            T.matmul(ps[:, M1, E:2 * E], tri[:, :], sel16[:, 1, :], start=False, stop=True)
            T.matmul(ps[:, M1, 2 * E:3 * E], ones[:, :], sel16[:, 0, :], start=True, stop=False)
            T.matmul(ps[:, M1, 2 * E:3 * E], ones[:, :], sel16[:, 1, :], start=False, stop=True).then_inc(pos_ps, 1)

            def gather():
                for h, banks in ((h_hi, (M0, M1)), (h_lo, (GB, SB_))):
                    for j, bank in enumerate(banks):
                        for m in range(4):
                            c = 4 * j + m
                            for b in range(NB):
                                ins = T.matmul(ps[:, bank, P * m:P * m + P], h[:, b, P * c:P * c + P], onehot[:, b, :],
                                               start=b == 0, stop=b == NB - 1)
                        ins.then_inc(gat_ps, 1)

            def scatter():
                for k, bank in enumerate((M0, M1, SB_, TB)):
                    b, half = divmod(k, 2)
                    o = slice(512 * half, 512 * half + 512)
                    T.matmul(ps[:, bank, :], onehotT[:, P * b:P * b + P], y_hi[:, o], start=True, stop=False)
                    T.matmul(ps[:, bank, :], onehotT[:, P * b:P * b + P], y_lo[:, o], start=False,
                             stop=True).then_inc(sc_ps, 1)

            pe.wait_ge(h_lo_ok, 2)
            pe.wait_ge(oh_ok, 2)
            pe.wait_ge(route_ok, 1)
            gather()

            total = T.value_load(passes.bitcast(I32), min_val=E, max_val=E + XP)
            T.sem_inc(et_ps, 1)
            with T.Fori(0, total) as p:
                def slot(j):
                    n = P_MOE + j
                    pe.wait_ge(lo_ready, p * PASS + (n + 1))
                    return w_hi[:, half_slot(n), :], w_lo[:, half_slot(n), :]

                def up_or_gate(j, bank, half):
                    wh, wl = (w.rearrange("p (c n) -> p c n", c=4) for w in slot(j))
                    for c in range(4):
                        ins = mm3(ps[:, bank, :], xt_hi[:, 4 * half + c, 0:P], xt_lo[:, 4 * half + c, 0:P],
                                  wh[:, c, :], wl[:, c, :], half == 0 and c == 0, half == 1 and c == 3)
                    ins.then_inc(piece_used, 1)

                def down_e(j, i, h):
                    wh, wl = (w.rearrange("p (s n) -> p s n", s=2) for w in slot(j))
                    for s in range(2):
                        for half, bank in enumerate((D0, D1)):
                            o = slice(512 * half, 512 * half + 512)
                            ins = mm3(ps[:, bank, :], eT_hi[i % 2][:, 2 * h + s, :], eT_lo[i % 2][:, 2 * h + s, :],
                                      wh[:, s, o], wl[:, s, o], (i, h, s) == (0, 0, 0), (i, h, s) == (EC - 1, 1, 1))
                    ins.then_inc(piece_used, 1)

                def turn_e(i):
                    pe.wait_ge(ea_ok, p * EC + (i + 2))
                    pe.wait_ge(el_ok, p * EC + (i + 1))
                    for s in range(4):
                        ins = T.transpose(ps[:, TB, P * s:P * s + P], act_e[:, P * s:P * s + P], ident[:, :])
                    ins.then_inc(et_ps, 1)

                for i in range(EC):
                    g0 = at(i)
                    pe.wait_ge(es_ok, p * EC + (i + 1))
                    if i == 0:
                        pe.wait_ge(gat_hi, p * 2 + 2)
                        pe.wait_ge(gat_lo, p * 2 + 2)
                    up_or_gate(g0, GB, 0)
                    up_or_gate(g0 + 1, GB, 1)
                    if i == 0:
                        pe.wait_ge(ys_lo, p + 1)
                        pe.wait_ge(oht_ok, p + 1)
                        pe.wait_ge(el_ok, p * EC + 1)
                        scatter()
                    else:
                        if i == 1:
                            pe.wait_ge(sc_ok, p * 4 + 4)
                            pe.wait_ge(oh_ok, p * 2 + 2)
                        turn_e(i - 1)
                        if i == 1:
                            for b in range(NB):
                                ins = T.transpose(ps[:, SB_, P * b:P * b + P], onehot[:, b, :].bitcast(F32), ident[:, :])
                            ins.then_inc(oht_ps, 1)
                    pe.wait_ge(ea_ok, p * EC + (i + 1))
                    up_or_gate(g0 + 2, UB, 0)
                    up_or_gate(g0 + 3, UB, 1)
                    if i == EC - 1:
                        pe.wait_ge(oh_ok, p * 2 + 4)
                        pe.wait_ge(es_ok, p * EC + (EC + 1))
                        pe.wait_ge(oht_ok, p + 2)
                        gather()
                    if i:
                        pe.wait_ge(el_ok, p * EC + (i + 1))
                        down_e(g0 + 4, i - 1, 0)
                        if i == EC - 1:
                            turn_e(i)
                        down_e(g0 + 5, i - 1, 1)
                pe.wait_ge(el_ok, p * EC + (EC + 1))
                down_e(PASS - 2, EC - 1, 0)
                down_e(PASS - 1, EC - 1, 1)
            pe.wait_ge(ys_lo, total + 1)
            pe.wait_ge(oht_ok, total + 1)
            pe.wait_ge(gat_hi, total * 2 + 2)
            pe.wait_ge(gat_lo, total * 2 + 2)
            pe.wait_ge(el_ok, total * EC + 1)
            scatter()


_INS = ["x", "norm_mix", "norm_ffn", "norm_final", "rel_bias", "attn_w_qkv", "attn_w_o", "attn_lambda_q1",
        "attn_lambda_k1", "attn_lambda_q2", "attn_lambda_k2", "attn_subln", "lru_w_in", "lru_conv_w", "lru_conv_b",
        "lru_gate_a_w", "lru_gate_a_b", "lru_gate_x_w", "lru_gate_x_b", "lru_lambda", "lru_w_out", "ffn_w_gate",
        "ffn_w_up", "ffn_w_down", "moe_router", "moe_w_gate", "moe_w_up", "moe_w_down"]


def kernel(**inputs):
    import numpy as _np
    import concourse.bacc as _bacc
    from concourse import mybir as _mybir
    from concourse.bass_utils import run_bass_kernel_spmd as _run

    nc = _bacc.Bacc("TRN2", target_bir_lowering=False, num_devices=1)
    arrays, args = {}, []
    for name in _INS:
        a = _np.ascontiguousarray(inputs[name])
        arrays[f"in_{name}_dram"] = a
        args.append(nc.dram_tensor(f"in_{name}_dram", a.shape, _mybir.dt.from_np(a.dtype), kind="ExternalInput").ap())
    out = nc.dram_tensor("out_0_dram", inputs["x"].shape, _mybir.dt.float32, kind="ExternalOutput").ap()
    build_trunk(nc, *args, out)
    r = _run(nc, [arrays], core_ids=[0])
    return r.results[0]["out_0_dram"]
```

```python
import math
from contextlib import ExitStack

import numpy as np

import concourse.bass as bass
from concourse import mybir

F32 = mybir.dt.float32
F32R = mybir.dt.float32r
BF16 = mybir.dt.bfloat16
I32 = mybir.dt.int32
ALU = mybir.AluOpType
ACT = mybir.ActivationFunctionType
AX_X = mybir.AxisListType.X

P = 128


def bucket_of(n, buckets, max_exact, max_distance):
    if n < max_exact:
        return n
    f = np.float32
    large = f(np.log(f(n) / f(max_exact))) / f(math.log(max_distance / max_exact)) * f(buckets - max_exact)
    return min(max_exact + int(large), buckets - 1)


def build_trunk(nc, x, norm_mix, norm_ffn, norm_final, rel_bias, w_qkv, w_o, lq1, lk1, lq2, lk2, subln,
                w_in, conv_w, conv_b, ga_w, ga_b, gx_w, gx_b, lam_p, w_out,
                f_gate, f_up, f_down, router, m_gate, m_up, m_down, out):
    _, S, D = x.shape
    NB = S // P
    KC = D // P
    HEADS = rel_bias.shape[1]
    BUCKETS = rel_bias.shape[0]
    HD = lq1.shape[1]
    VD = 2 * HD
    SCALE = HD ** -0.5
    LAM_INIT = 0.8 - 0.6 * math.exp(0.0)
    R = w_out.shape[1]
    RB = R // P
    FF = f_gate.shape[2]
    E = m_gate.shape[1]
    FE = m_gate.shape[3]
    CW = 512
    EC = FE // CW
    FC = FF // CW
    XP = 3
    NEG = -1e30
    assert (S, D, VD, FE % CW, FF - FC * CW, RB % 2) == (256, 1024, P, 0, 256, 0)
    assert P + (2 * S - 1) // P <= P + XP and (XP + 1) * (P + 1) > 2 * S

    PIECE = 2048

    def cols4(w, half, c0):
        return w.rearrange("(c p) n -> p c n", p=P)[:, 4 * half:4 * half + 4, c0:c0 + 512]

    def cols8(w, c0):
        return w.rearrange("(c p) n -> p c n", p=P)[:, :, c0:c0 + 256]

    def rows2(w, r0):
        return w[r0:r0 + 256, :].rearrange("(s p) n -> p s n", p=P)

    static = []
    wq = w_qkv[0]
    for part in range(2):
        qk = [[cols8(wq, 512 * part + 256 * pair), cols8(wq, D + 512 * part + 256 * pair)] for pair in range(2)]
        vs = [cols4(wq, h, 2 * D + 512 * part) for h in range(2)]
        static += qk[0] + vs + qk[1]
    P_WO = len(static)
    static += [cols4(w_o[0], h, 512 * g) for h in range(2) for g in range(2)]
    P_FFN = len(static)
    fg, fu, fd = f_gate[0], f_up[0], f_down[0]
    for i in range(FC):
        static += [cols4(fg, h, CW * i) for h in range(2)]
        if i:
            static += [rows2(fd, CW * (i - 1) + 256 * h) for h in range(2)]
        static += [cols4(fu, h, CW * i) for h in range(2)]
    static += [cols8(fg, CW * FC)] + [rows2(fd, CW * (FC - 1) + 256 * h) for h in range(2)]
    static += [cols8(fu, CW * FC), rows2(fd, CW * FC)]

    def f_gate_at(i):
        return P_FFN + (0 if i == 0 else 6 * i - 2)

    def f_up_at(i):
        return P_FFN + 2 if i == 0 else f_gate_at(i) + (4 if i < FC else 3)

    def f_down_at(i):
        return f_gate_at(i + 1) + (2 if i + 1 < FC else 1) if i < FC else f_up_at(FC) + 1
    P_IN = len(static)
    static += [cols8(w_in[0], R + 256 * j) for j in range(RB // 2)]
    static += [cols8(w_in[0], 256 * j) for j in range(RB // 2)]
    P_OUT = len(static)
    static += [rows2(w_out[0], 256 * j) for j in range(RB // 2)]
    P_MOE = len(static)
    PASS = EC * 6

    XR, WR, HR = 3, 4, 4
    assert PASS % (XR + WR) == 0 and P_MOE % WR == 0
    HALF = [s for size in (4, 4, 4, 3, 4, 4, 4, 4, 3, 4, 4) for s in range(size)]
    assert len(HALF) == PASS

    def land_slot(n):
        return XR + n % WR if n < P_MOE else (n - P_MOE) % (XR + WR)

    def land_back(n):
        return WR if n < P_MOE else XR + WR

    def landings(n):
        return sum(land_slot(m) == land_slot(n) for m in range(n + 1))

    LANDINGS = PASS // (XR + WR)

    def half_slot(n):
        return HALF[(n - P_MOE) % PASS]

    def half_back(n):
        return next(d for d in range(1, PASS) if half_slot(n - d) == half_slot(n))

    mg = m_gate.rearrange("a e (c p) f -> (a e) p c f", p=P)
    mu = m_up.rearrange("a e (c p) f -> (a e) p c f", p=P)
    md = m_down.rearrange("a e (s p) n -> (a e) p s n", p=P)

    def expert_pieces(e):
        pieces = []
        for i in range(EC):
            pieces += [mg[e, :, 4 * h:4 * h + 4, CW * i:CW * i + CW] for h in range(2)]
            pieces += [mu[e, :, 4 * h:4 * h + 4, CW * i:CW * i + CW] for h in range(2)]
            if i:
                pieces += [md[e, :, 4 * (i - 1) + 2 * h:4 * (i - 1) + 2 * h + 2, :] for h in range(2)]
        pieces += [md[e, :, 4 * (EC - 1) + 2 * h:4 * (EC - 1) + 2 * h + 2, :] for h in range(2)]
        return pieces

    def at(i):
        return 0 if i == 0 else 4 + 6 * (i - 1)

    rel_scratch = nc.dram_tensor("rel_scratch", [HEADS, 3 * P], F32).ap()

    with ExitStack() as ctx:
        def sb(name, shape, dt=F32):
            return ctx.enter_context(nc.sbuf_tensor(name, shape, dt))

        def sem(name):
            return ctx.enter_context(nc.semaphore(name))

        w_ring = sb("w_ring", [P, WR, PIECE])
        w_hi = sb("w_hi", [P, HR, PIECE], F32R)
        w_lo = sb("w_lo", [P, HR, PIECE], F32R)
        xres = sb("xres", [P, NB, D])
        hn = sb("hn", [P, NB, D])
        gain = sb("gain", [P, D])
        xt_hi = sb("xt_hi", [P, KC, S], F32R)
        xt_lo = sb("xt_lo", [P, KC, S], F32R)
        split = sb("split", [P, 7680], F32R)
        work = sb("work", [P, 10760])
        ident = sb("ident", [P, P])
        iota_s = sb("iota_s", [P, P])
        tri = sb("tri", [P, P], BF16)
        ones = sb("ones", [P, P], BF16)
        rw = sb("rw", [P, KC, E])
        small = sb("small", [P, 376])
        neg_lam = small[:, 0:1]
        ss = small[:, 2:4]
        rstd = small[:, 4:6]
        nt = small[:, 6:8]
        lam_e = small[:, 10:12]
        ntmp = small[:, 12:14]
        sd = small[:, 8:10]
        prm = small[:, 16:96]
        cvw = prm[:, 0:4 * RB].rearrange("p (j n) -> p j n", j=4)
        cvb = prm[:, 4 * RB:5 * RB]
        gab = prm[:, 5 * RB:6 * RB]
        gxb = prm[:, 6 * RB:7 * RB]
        lamp = prm[:, 7 * RB:8 * RB]
        decay = small[:, 96:96 + RB]
        decay2 = small[:, 360:360 + RB]
        warm = small[:, 370:375]
        lt = small[:, 110:110 + 5 * RB].rearrange("p (k n) -> p k n", k=5)
        mx = small[:, 160:168].rearrange("p (h k) -> p h k", h=2)
        es = small[:, 168:176].rearrange("p (h k) -> p h k", h=2)
        er = small[:, 176:184].rearrange("p (h k) -> p h k", h=2)
        oss = small[:, 184:248].rearrange("p (k n) -> p k n", k=4)
        g_cur = small[:, 248:250]
        c_cur = small[:, 250:252]
        slots = small[:, 252:252 + NB * (E + XP + 1)].rearrange("p (b n) -> p b n", b=NB)
        combs = small[:, 276:276 + NB * (E + XP + 2)].rearrange("p (b n) -> p b n", b=NB)
        passes = small[0:1, 310:311]
        extra = small[0:1, 312:312 + XP]
        iota_e = small[:, 320:328]
        counts = small[:, 328:336]
        ranks = small[:, 336:344]
        pick = small[:, 344:352]

        qT = work[:, 0:2048].rearrange("p (h t) -> p h t", h=HEADS)
        kT = work[:, 2048:4096].rearrange("p (h t) -> p h t", h=HEADS)
        v = work[:, 4096:6144].rearrange("p (b n) -> p b n", b=NB)
        bias = work[:, 6144:8192].rearrange("p (h t) -> p h t", h=HEADS)
        ex = work[:, 8192:9728].rearrange("p (h c n) -> p h c n", h=2, c=2)
        aT = work[:, 9728:10496].rearrange("p (h n) -> p h n", h=2)
        subln_b = work[:, 10496:10624]
        lamv = work[:, 9728:9984].rearrange("p (k n) -> p k n", k=4)
        rows_in = work[:, 9984:10112]
        rel_in = work[:, 10112:10120]
        relT = work[0:HEADS, 10120:10152]
        lamj = work[:, 10152:10216]
        o_sq = gain[:, :].rearrange("p (b h e) -> p b h e", b=NB, h=4)
        rel_row = work[0:HEADS, 8192:8192 + 3 * P]
        flip = work[:, 10240:10368]
        bias_up = work[:, 4096:6144]
        act_f = work[:, 0:1024].rearrange("p (b n) -> p b n", b=NB)
        aT_hi = split[:, 0:1024].rearrange("p (s t) -> p s t", s=4)
        aT_lo = split[:, 1024:2048].rearrange("p (s t) -> p s t", s=4)
        rt = work[:, 0:2560].rearrange("p (n t) -> p n t", n=RB)
        ix = work[:, 2560:5120].rearrange("p (n t) -> p n t", n=RB)
        ra = work[:, 5120:7680].rearrange("p (n t) -> p n t", n=RB)
        gate = work[:, 0:2560].rearrange("p (n t) -> p n t", n=RB)
        wga = work[:, 7680:8960].rearrange("p (n e) -> p n e", n=RB)
        wgx = work[:, 8960:10240].rearrange("p (n e) -> p n e", n=RB)
        hs = work[:, 7680:10240].rearrange("p (n t) -> p n t", n=RB)
        xb = work[:, 10240:10240 + 2 * 259].rearrange("p (n t) -> p n t", n=2)
        xc = hn[:, 0, :].rearrange("p (j n t) -> p j n t", j=2, n=2)
        ig = hn[:, 1, 512:1024].rearrange("p (n t) -> p n t", n=2)
        yT_hi = split[:, 0:2560].rearrange("p (n t) -> p n t", n=RB)
        yT_lo = split[:, 2560:5120].rearrange("p (n t) -> p n t", n=RB)
        act_e = work[:, 0:512]
        xtf = work[:, 0:2048] .rearrange("p (c t) -> p c t", c=KC)
        rt_b = [work[:, 2048 + 16 * k:2064 + 16 * k].rearrange("p (b e) -> p b e", b=NB) for k in range(12)]
        h_hi = split[:, 0:2048].rearrange("p (b n) -> p b n", b=NB)
        h_lo = split[:, 2048:4096].rearrange("p (b n) -> p b n", b=NB)
        y_hi = split[:, 4096:5120]
        y_lo = split[:, 5120:6144]
        onehot = split[:, 6144:6400].rearrange("p (b s) -> p b s", b=NB)
        onehotT = split[:, 6400:6656]
        eT_hi = [split[:, 6656:7168].rearrange("p (s t) -> p s t", s=4), xt_hi[:, 0:4, P:2 * P]]
        eT_lo = [split[:, 7168:7680].rearrange("p (s t) -> p s t", s=4), xt_lo[:, 0:4, P:2 * P]]
        x_ring = work[:, 2560:2560 + XR * PIECE].rearrange("p (k n) -> p k n", k=XR)

        def land(n):
            s = land_slot(n)
            return x_ring[:, s, :] if s < XR else w_ring[:, s - XR, :]

        sel16 = sb("sel16", [P, NB, E], BF16)

        ps = ctx.enter_context(nc.psum_tensor("ps", [P, 8, 512], F32))
        GB, UB, TB, SB_, M0, M1, D0, D1 = range(8)
        GATE_BANKS = (6, 7, 1, 0, 6)

        landed = [sem(f"landed{s}") for s in range(XR + WR)]
        hi_ready, lo_ready, piece_used = sem("hi_ready"), sem("lo_ready"), sem("piece_used")
        in_x, in_table = [sem(f"in_x{b}") for b in range(NB)], sem("in_table")
        in_small, in_gain, in_lru, in_rel, rel_out = (sem("in_small"), sem("in_gain"),
                                                            sem("in_lru"), sem("in_rel"), sem("rel_out"))
        consts, late_consts = sem("consts"), sem("late_consts")
        dve_link, act_link, pool_link = sem("dve_link"), sem("act_link"), sem("pool_link")
        x_ready, sq_ready, var_ready, root_ready, hn_ready = (sem("x_ready"), sem("sq_ready"), sem("var_ready"),
                                                              sem("root_ready"), sem("hn_ready"))
        xt_ps, xt_hi_ok, xt_lo_ok = sem("xt_ps"), sem("xt_hi_ok"), sem("xt_lo_ok")
        prm_ps, prm_ok, rel_ps, rel_row_ok = sem("prm_ps"), sem("prm_ok"), sem("rel_ps"), sem("rel_row_ok")
        flip_ps, bias_ok = sem("flip_ps"), sem("bias_ok")
        lam_dot, lam_exp, decay_in = sem("lam_dot"), sem("lam_exp"), sem("decay_in")
        q_out, k_out, v_out_a, v_out_d = sem("q_out"), sem("k_out"), sem("v_out_a"), sem("v_out_d")
        s_done, masked, exp_done, probs = sem("s_done"), sem("masked"), sem("exp_done"), sem("probs")
        t_done, aT_ok, o_done, o_out = sem("t_done"), sem("aT_ok"), sem("o_done"), sem("o_out")
        ovar, oroot, on_ready = sem("ovar"), sem("oroot"), sem("on_ready")
        fs, fa, ft, fh, fl = sem("f_silu"), sem("f_act"), sem("f_tr"), sem("f_hi"), sem("f_lo")
        xb_zero, gexp_in, gexp_ok = sem("xb_zero"), sem("gexp_in"), sem("gexp_ok")
        cur_ok = sem("cur_ok")
        xb_ok, xc_ok, ri_ps, ri_ok, ix_ok = sem("xb_ok"), sem("xc_ok"), sem("ri_ps"), sem("ri_ok"), sem("ix_ok")
        a_ok = sem("a_ok")
        t_ok, sqt_ok, gelu_ok, y_ok, yh_ok, yl_ok = (sem("t_ok"), sem("sqt_ok"), sem("gelu_ok"), sem("y_ok"),
                                                     sem("yh_ok"), sem("yl_ok"))
        xtf_a, xtf_d, log_ps, sel_ok, pos_ps, route_ok = (sem("xtf_a"), sem("xtf_d"), sem("log_ps"), sem("sel_ok"),
                                                          sem("pos_ps"), sem("route_ok"))
        dl_ok, de_ok, h_hi_ok, h_lo_ok = sem("dl_ok"), sem("de_ok"), sem("h_hi_ok"), sem("h_lo_ok")
        oh_ok, oht_ps, oht_ok = sem("oh_ok"), sem("oht_ps"), sem("oht_ok")
        gat_ps, gat_hi, gat_lo = sem("gat_ps"), sem("gat_hi"), sem("gat_lo")
        es_ok, ea_ok, et_ps, eh_ok, el_ok = sem("es_ok"), sem("ea_ok"), sem("et_ps"), sem("eh_ok"), sem("el_ok")
        ys_hi, ys_lo, sc_ps, sc_ok, out_done = sem("ys_hi"), sem("ys_lo"), sem("sc_ps"), sem("sc_ok"), sem("out_done")

        block = ctx.enter_context(nc.Block())

        @block.sync
        def _(sp):
            for b in range(NB):
                sp.dma_start(xres[:, b, :], x[0, b * P:(b + 1) * P, :]).then_inc(in_x[b], 16)
            sp.dma_start(gain[:, :], norm_mix[0:1, :].to_broadcast([P, D])).then_inc(in_gain, 16)

            def load(n, src, uses=0):
                if n >= WR:
                    sp.wait_ge(lo_ready, uses * PASS + (n - land_back(n) + 1))
                dst = land(n)[:, 0:src.shape[1] * src.shape[2]]
                sp.dma_start(dst.rearrange("p (c n) -> p c n", c=src.shape[1]), src).then_inc(landed[land_slot(n)], 16)

            for n in range(WR):
                load(n, static[n])
            for n in range(WR, P_MOE):
                if n == P_FFN + 3:
                    sp.wait_ge(on_ready, 2)
                    sp.dma_start(gain[:, :], norm_ffn[0:1, :].to_broadcast([P, D])).then_inc(in_gain, 16)
                if n == P_IN - 3:
                    sp.wait_ge(hn_ready, 4)
                    sp.dma_start(gain[:, :], norm_mix[1:2, :].to_broadcast([P, D])).then_inc(in_gain, 16)
                    sp.dma_start(wga, ga_w[0].rearrange("n d e -> d n e")).then_inc(in_lru, 16)
                    sp.dma_start(wgx, gx_w[0].rearrange("n d e -> d n e")).then_inc(in_lru, 16)
                if n == P_OUT:
                    sp.wait_ge(hn_ready, 6)
                    sp.dma_start(gain[:, :], norm_ffn[1:2, :].to_broadcast([P, D])).then_inc(in_gain, 16)
                load(n, static[n])

            sp.wait_ge(y_ok, 2)
            with nc.sync.Fori(0, E) as p:
                for j, src in enumerate(expert_pieces(p)):
                    load(P_MOE + j, src, uses=p)
            sp.wait_ge(hn_ready, 8)
            sp.dma_start(gain[:, :], norm_final.rearrange("(a n) -> a n", a=1).to_broadcast([P, D])).then_inc(in_gain, 16)
            sp.wait_ge(route_ok, 1)
            total = nc.sync.value_load(passes.bitcast(I32), min_val=E, max_val=E + XP)
            with nc.sync.If(total > E):
                with nc.sync.Fori(E, total) as p:
                    e = nc.sync.value_load(small[0:1, bass.ds(p + (312 - E), 1)].bitcast(I32), min_val=0,
                                           max_val=E - 1)
                    for j, src in enumerate(expert_pieces(e)):
                        load(P_MOE + j, src, uses=p)
            for b in range(NB):
                sp.wait_ge(hn_ready, 9 + b)
                sp.dma_start(out[0, b * P:(b + 1) * P, :], hn[:, b, :]).then_inc(out_done, 16)
            sp.wait_ge(out_done, 16 * NB)

        @block.gpsimd
        def _(pool):
            nc.gpsimd.memset(ident[:, :], 0.0).then_inc(pool_link, 1)
            nc.gpsimd.memset(flip, 0.0).then_inc(pool_link, 1)
            nc.gpsimd.memset(tri[:, :], 0.0).then_inc(pool_link, 1)
            pool.wait_ge(pool_link, 3)
            nc.gpsimd.affine_select(out=ident[:, :], in_=ident[:, :], compare_op=ALU.not_equal, fill=1.0,
                                    base=0, pattern=[[-1, P]], channel_multiplier=1).then_inc(consts, 1)
            nc.gpsimd.affine_select(out=flip, in_=flip, compare_op=ALU.not_equal, fill=1.0,
                                    base=1 - P, pattern=[[1, P]], channel_multiplier=1).then_inc(consts, 1)
            with nc.allow_non_contiguous_dma(reason="small parameters"):
                pool.dma_start(rel_in[0:BUCKETS, :], rel_bias).then_inc(in_table, 16)
                rows = [(conv_w[0, j].rearrange("(n p) -> n p", p=P), RB) for j in range(4)]
                rows += [(a[0].rearrange("(n p) -> n p", p=P), RB) for a in (conv_b, ga_b, gx_b, lam_p)]
                for k, (src, n) in enumerate(rows):
                    pool.dma_start(rows_in[k * RB:k * RB + n, :], src).then_inc(in_small, 16)
                for k, a in enumerate((lq1, lk1, lq2, lk2)):
                    pool.dma_start(lamv[:, k, :], a[0:1, :].to_broadcast([P, HD])).then_inc(in_small, 16)
                pool.dma_start(subln_b, subln[0:1, :].to_broadcast([P, VD])).then_inc(in_small, 16)
                pool.dma_start(rw[:, :, :], router[0].rearrange("(c p) e -> p c e", p=P)).then_inc(in_small, 16)
            pool.wait_ge(rel_row_ok, 1)
            pool.dma_start(rel_scratch, rel_row).then_inc(rel_out, 16)
            pool.wait_ge(rel_out, 16)
            skew = bass.AP(rel_scratch.tensor, 0, [[1, P], [3 * P, HEADS], [1, S]])
            pool.dma_start(bias_up, skew).then_inc(in_rel, 16)
            nc.gpsimd.affine_select(out=tri[:, :], in_=tri[:, :], compare_op=ALU.is_ge, fill=1.0,
                                    base=0, pattern=[[-1, P]], channel_multiplier=1).then_inc(late_consts, 1)
            nc.gpsimd.memset(ones[:, :], 1.0).then_inc(late_consts, 1)
            nc.gpsimd.iota(iota_s[:, :], pattern=[[1, P]], base=0, channel_multiplier=0,
                           allow_small_or_imprecise_dtypes=True).then_inc(late_consts, 1)
            nc.gpsimd.iota(iota_e, pattern=[[1, E]], base=0, channel_multiplier=0,
                           allow_small_or_imprecise_dtypes=True).then_inc(late_consts, 1)

        @block.scalar
        def _(act):
            links = [0]
            done = [0]

            def copy(out, in_):
                return nc.scalar.activation(out, in_, ACT.Copy)

            def hi_upto(n):
                while done[0] <= n:
                    k = done[0]
                    act.wait_ge(landed[land_slot(k)], 16 * landings(k))
                    if k >= half_back(k):
                        act.wait_ge(piece_used, k - half_back(k) + 1)
                    copy(w_hi[:, half_slot(k), :], land(k)).then_inc(hi_ready, 1)
                    done[0] += 1

            def square_sums(t):
                if t:
                    nc.scalar.activation(warm[:, t:t + 1], nt[:, 0:1], ACT.Sqrt)
                else:
                    act.wait_ge(consts, 1)
                    nc.scalar.activation(warm[:, 0:1], ident[:, 0:1], ACT.Sqrt)
                for b in range(NB):
                    if t:
                        act.wait_ge(x_ready, 2 * (t - 1) + b + 1)
                    else:
                        act.wait_ge(in_x[b], 16)
                    nc.scalar.activation(hn[:, b, :], xres[:, b, :], ACT.Square,
                                         accum_out=ss[:, b:b + 1]).then_inc(sq_ready, 1)

            def root(t):
                act.wait_ge(var_ready, t + 1)
                nc.scalar.activation(sd, nt, ACT.Sqrt).then_inc(root_ready, 1)

            def xt_split(count, banks, c0):
                for j, b in enumerate(banks):
                    act.wait_ge(xt_ps, count + j + 1)
                    copy(xt_hi[:, c0 + 2 * j:c0 + 2 * j + 2, :],
                         ps[:, b, :].rearrange("p (c t) -> p c t", c=2)).then_inc(xt_hi_ok, 1)

            def exps(h):
                act.wait_ge(masked, 4 * (h + 1))
                for c in range(2):
                    for b in range(2):
                        seg = ex[:, h % 2, c, 256 * (1 - b):256 + 128 * (1 - b)]
                        k = 2 * c + b
                        nc.scalar.activation(seg, seg, ACT.Exp, bias=mx[:, h % 2, k:k + 1], scale=-1.0,
                                             accum_out=es[:, h % 2, k:k + 1]).then_inc(exp_done, 1)

            def aT_out(h):
                act.wait_ge(t_done, h + 1)
                if h >= 2:
                    act.wait_ge(o_done, h - 1)
                copy(aT[:, h % 2, :], ps[:, 2, 0:384]).then_inc(aT_ok, 1)

            def o_evac(h):
                act.wait_ge(o_done, h + 1)
                copy(hn[:, :, P * h:P * h + P],
                     ps[:, 3, 0:256].rearrange("p (b n) -> p b n", b=NB)).then_inc(o_out, 1)

            def q_evac(n, k):
                act.wait_ge(piece_used, n + 1)
                copy(qT[:, 2 * k:2 * k + 2, :], ps[:, 0, :].rearrange("p (h t) -> p h t", h=2)).then_inc(q_out, 1)

            def v_evac(n, part):
                act.wait_ge(piece_used, n + 1)
                copy(v[:, 0, 512 * part:512 * part + 512], ps[:, 0, :]).then_inc(v_out_a, 1)

            def head_root(k):
                act.wait_ge(ovar, k + 1)
                nc.scalar.activation(oss[:, 1, 8 * k:8 * k + 8], oss[:, 0, 8 * k:8 * k + 8],
                                     ACT.Sqrt).then_inc(oroot, 1)

            square_sums(0)
            root(0)
            hi_upto(0)
            xt_split(0, range(4), 0)
            hi_upto(3)
            q_evac(0, 0)
            hi_upto(6)
            v_evac(3, 0)
            hi_upto(7)
            act.wait_ge(lam_dot, 2)
            nc.scalar.activation(lam_e, lam_e, ACT.Exp).then_inc(lam_exp, 1)
            exps(0)
            q_evac(4, 1)
            aT_out(0)
            exps(1)
            hi_upto(8)
            hi_upto(9)
            o_evac(0)
            aT_out(1)
            exps(2)
            q_evac(6, 2)
            hi_upto(10)
            o_evac(1)
            aT_out(2)
            exps(3)
            hi_upto(11)
            o_evac(2)
            aT_out(3)
            exps(4)
            hi_upto(12)
            o_evac(3)
            aT_out(4)
            exps(5)
            v_evac(9, 1)
            hi_upto(13)
            head_root(0)
            q_evac(10, 3)
            o_evac(4)
            aT_out(5)
            hi_upto(14)
            o_evac(5)
            exps(6)
            xt_split(4, (6, 7), 0)
            exps(7)
            hi_upto(15)
            aT_out(6)
            o_evac(6)
            aT_out(7)
            o_evac(7)
            head_root(1)
            xt_split(6, (2, 3), 4)
            hi_upto(16)
            act.wait_ge(dl_ok, 1)
            nc.scalar.activation(lt[:, 1, :], lt[:, 0, :], ACT.Exp, scale=-1.0).then_inc(de_ok, 1)
            hi_upto(P_FFN + 2)
            square_sums(1)
            root(1)
            xt_split(8, range(4), 0)

            def aT_split_hi(k, subs):
                act.wait_ge(ft, k + 1)
                b = k % 2
                copy(aT_hi[:, 0:subs, P * b:P * b + P],
                     ps[:, 2 + b, 0:P * subs].rearrange("p (s t) -> p s t", s=subs)).then_inc(fh, 1)

            for i in range(FC + 1):
                last = i == FC
                hi_upto(f_gate_at(i) + 2)
                if i:
                    aT_split_hi(2 * i - 2, 4)
                    aT_split_hi(2 * i - 1, 4)
                hi_upto(f_gate_at(i) + (2 if last else 3))
                act.wait_ge(piece_used, f_gate_at(i) + (1 if last else 2))
                for b in range(NB):
                    cols = 256 if last else CW
                    nc.scalar.activation(act_f[:, b, 0:cols], ps[:, b, 0:cols], ACT.Silu).then_inc(fs, 1)
            hi_upto(P_IN + 1)
            aT_split_hi(2 * FC, 2)
            aT_split_hi(2 * FC + 1, 2)

            hi_upto(P_IN + 2)
            square_sums(2)
            root(2)
            xt_split(12, range(4), 0)
            def recurrence_gates(j):
                act.wait_ge(ri_ps, j + 1)
                if j:
                    act.wait_ge(ix_ok, j)
                else:
                    act.wait_ge(decay_in, 2)
                for m in range(2):
                    b = 2 * j + m
                    nc.scalar.activation(ig[:, m, :], ps[:, 3, 256 * m:256 * m + 256], ACT.Sigmoid,
                                         bias=gxb[:, b:b + 1]).then_inc(ri_ok, 1)
                    nc.scalar.activation(ra[:, b, :], ps[:, 2, 256 * m:256 * m + 256], ACT.Sigmoid,
                                         bias=gab[:, b:b + 1]).then_inc(act_link, 1)
                    links[0] += 1
                act.wait_ge(act_link, links[0])
                for m in range(2):
                    b = 2 * j + m
                    nc.scalar.activation(rt[:, b, :], ra[:, b, :], ACT.Tanh,
                                         scale=decay[:, b:b + 1]).then_inc(t_ok, 1)
            for j in range(RB // 2):
                act.wait_ge(piece_used, P_IN + j + 1)
                if j:
                    act.wait_ge(xc_ok, j)
                else:
                    act.wait_ge(xb_zero, 1)
                copy(xb[:, :, 3:3 + S], ps[:, j % 2, :].rearrange("p (n t) -> p n t", n=2)).then_inc(xb_ok, 1)
                if j:
                    recurrence_gates(j - 1)
                hi_upto(P_IN + j + 3)
            hi_upto(P_IN + RB // 2 + 3)
            recurrence_gates(RB // 2 - 1)
            act.wait_ge(t_ok, RB)
            for b in range(RB):
                nc.scalar.activation(ra[:, b, :], ra[:, b, :], ACT.Exp, scale=decay2[:, b:b + 1]).then_inc(a_ok, 1)
            for g in range(2):
                n0, n1 = g * RB // 2, (g + 1) * RB // 2
                nc.scalar.activation(hs[:, n0:n1, :], rt[:, n0:n1, :], ACT.Sqrt, scale=-1.0).then_inc(sqt_ok, 1)
            act.wait_ge(sqt_ok, 2)
            for j in range(RB // 2):
                act.wait_ge(piece_used, P_IN + RB // 2 + j + 1)
                nc.scalar.activation(gate[:, 2 * j:2 * j + 2, :], ps[:, GATE_BANKS[j], :].rearrange("p (n t) -> p n t", n=2),
                                     ACT.Gelu_apprx_tanh).then_inc(gelu_ok, 1)
                hi_upto(P_IN + RB // 2 + j + 3)
            for j in range(RB // 2):
                act.wait_ge(y_ok, j + 1)
                copy(yT_hi[:, 2 * j:2 * j + 2, :], gate[:, 2 * j:2 * j + 2, :]).then_inc(yh_ok, 1)
                hi_upto(P_OUT + j + 2)

            hi_upto(P_MOE - 1)
            square_sums(3)
            root(3)
            for j in range(0, 4, 2):
                act.wait_ge(xt_ps, 16 + j + 1)
                copy(xtf[:, 2 * j:2 * j + 2, :], ps[:, j, :].rearrange("p (c t) -> p c t", c=2)).then_inc(xtf_a, 1)
            hi_upto(P_MOE)
            act.wait_ge(hn_ready, 8)
            act.wait_ge(piece_used, P_MOE)
            for b in range(NB):
                copy(h_hi[:, b, :], hn[:, b, :]).then_inc(h_hi_ok, 1)
            hi_upto(P_MOE + 1)
            act.wait_ge(gexp_in, 1)
            nc.scalar.activation(rt_b[8][:, :, 1:2], rt_b[8][:, :, 0:1], ACT.Exp).then_inc(gexp_ok, 1)
            hi_upto(P_MOE + HR - 1)

            def gathered_hi(count):
                for j, b in enumerate((M0, M1)):
                    act.wait_ge(gat_ps, count + j + 1)
                    copy(xt_hi[:, 4 * j:4 * j + 4, 0:P], ps[:, b, :].rearrange("p (c t) -> p c t", c=4)).then_inc(gat_hi, 1)

            gathered_hi(0)
            nc.scalar.sem_inc(es_ok, 1)
            def expert(p):
                def hi(j):
                    if isinstance(p, int) and j < HR:
                        return
                    n = P_MOE + j
                    act.wait_ge(landed[land_slot(n)], p * (16 * LANDINGS) + 16 * landings(n))
                    act.wait_ge(piece_used, p * PASS + (n - half_back(n) + 1))
                    copy(w_hi[:, half_slot(n), :], land(n)).then_inc(hi_ready, 1)

                def eT_split_hi(i):
                    act.wait_ge(et_ps, p * EC + (i + 2))
                    copy(eT_hi[i % 2], ps[:, TB, :].rearrange("p (s t) -> p s t", s=4)).then_inc(eh_ok, 1)

                def silu(i):
                    act.wait_ge(piece_used, p * PASS + (P_MOE + at(i) + 2))
                    act.wait_ge(et_ps, p * EC + (i + 1))
                    nc.scalar.activation(act_e, ps[:, GB, :], ACT.Silu).then_inc(es_ok, 1)

                hi(0)
                hi(1)
                act.wait_ge(piece_used, p * PASS + P_MOE)
                copy(y_hi, ps[:, D0:D0 + 2, :].rearrange("p a n -> p (a n)")).then_inc(ys_hi, 1)
                hi(2)
                hi(3)
                hi(4)
                silu(0)
                for i in range(1, EC):
                    g0 = at(i)
                    for j in range(0 if i > 1 else 1, 6):
                        hi(g0 + j)
                    eT_split_hi(i - 1)
                    silu(i)
                hi(PASS - 2)
                hi(PASS - 1)
                for j, b in enumerate((M0, M1)):
                    act.wait_ge(gat_ps, p * 4 + (4 + j + 1))
                    copy(xt_hi[:, 4 * j:4 * j + 4, 0:P],
                         ps[:, b, :].rearrange("p (c t) -> p c t", c=4)).then_inc(gat_hi, 1)
                eT_split_hi(EC - 1)

            expert(0)
            act.wait_ge(route_ok, 1)
            total = nc.scalar.value_load(passes.bitcast(I32), min_val=E, max_val=E + XP)
            with nc.scalar.Fori(1, total) as p:
                expert(p)
            act.wait_ge(piece_used, total * PASS + P_MOE)
            copy(y_hi, ps[:, D0:D0 + 2, :].rearrange("p a n -> p (a n)")).then_inc(ys_hi, 1)
            nc.scalar.activation(warm[:, 4:5], nt[:, 0:1], ACT.Sqrt)
            for b in range(NB):
                act.wait_ge(sc_ok, total * 4 + (2 * b + 2))
                nc.scalar.activation(hn[:, b, :], xres[:, b, :], ACT.Square, accum_out=ss[:, b:b + 1]).then_inc(sq_ready, 1)
            root(4)

        @block.vector
        def _(dve):
            links = [0]
            done = [0]
            V = nc.vector

            def link(ins):
                links[0] += 1
                ins.then_inc(dve_link, 1)
                dve.wait_ge(dve_link, links[0])

            def lo_upto(n):
                while done[0] <= n:
                    k = done[0]
                    dve.wait_ge(hi_ready, k + 1)
                    V.tensor_tensor(w_lo[:, half_slot(k), :], land(k), w_hi[:, half_slot(k), :].bitcast(F32),
                                    ALU.subtract).then_inc(lo_ready, 1)
                    done[0] += 1

            def rsqrt(out, var, root_of, tmp, step=link):
                step(V.reciprocal(out, root_of))
                step(V.tensor_tensor(tmp, out, out, ALU.mult))
                step(V.tensor_tensor(tmp, tmp, var, ALU.mult))
                step(V.tensor_scalar(tmp, tmp, -0.5, 1.5, ALU.mult, ALU.add))
                step(V.tensor_tensor(out, out, tmp, ALU.mult))

            def norm(t):
                dve.wait_ge(sq_ready, 2 * t + 2)
                V.tensor_scalar(nt, ss, 1.0 / D, 1e-6, ALU.mult, ALU.add).then_inc(var_ready, 1)
                dve.wait_ge(var_ready, t + 1)
                dve.wait_ge(root_ready, t + 1)
                rsqrt(rstd, nt, sd, ntmp)
                dve.wait_ge(in_gain, 16 * (t + 1))
                for b in range(NB):
                    V.scalar_tensor_tensor(hn[:, b, :], xres[:, b, :], rstd[:, b:b + 1], gain[:, :],
                                           ALU.mult, ALU.mult).then_inc(hn_ready, 1)

            def xt_split(count, banks, c0):
                for j, b in enumerate(banks):
                    dve.wait_ge(xt_hi_ok, count + j + 1)
                    V.tensor_tensor(xt_lo[:, c0 + 2 * j:c0 + 2 * j + 2, :], ps[:, b, :].rearrange("p (c t) -> p c t", c=2),
                                    xt_hi[:, c0 + 2 * j:c0 + 2 * j + 2, :].bitcast(F32),
                                    ALU.subtract).then_inc(xt_lo_ok, 1)

            def mask(h):
                dve.wait_ge(s_done, h + 1)
                if h == 0:
                    dve.wait_ge(bias_ok, 1)
                if h >= 2:
                    dve.wait_ge(t_done, h - 1)
                for c in range(2):
                    for b in range(2):
                        n0, n1 = 256 * (1 - b), 256 + 128 * (1 - b)
                        k = 2 * c + b
                        V.tensor_tensor_reduce(out=ex[:, h % 2, c, n0:n1], in0=ps[:, 4 + c, n0:n1],
                                               in1=bias[:, h, P * (1 - b):S], scale=-SCALE, scalar=3e38, op0=ALU.add,
                                               op1=ALU.min, accum_out=mx[:, h % 2, k:k + 1]).then_inc(masked, 1)

            def mix(h):
                dve.wait_ge(exp_done, 4 * (h + 1))
                r, e = er[:, h % 2], ex[:, h % 2]
                link(V.reciprocal(r, es[:, h % 2]))
                link(V.tensor_scalar(r[:, 2:4], r[:, 2:4], neg_lam, None, ALU.mult))
                V.tensor_scalar(e[:, 0, 0:256], e[:, 0, 0:256], r[:, 1:2], None, ALU.mult)
                link(V.tensor_scalar(e[:, 0, 256:384], e[:, 0, 256:384], r[:, 0:1], None, ALU.mult))
                V.scalar_tensor_tensor(e[:, 0, 0:256], e[:, 1, 0:256], r[:, 3:4], e[:, 0, 0:256], ALU.mult, ALU.add)
                V.scalar_tensor_tensor(e[:, 0, 256:384], e[:, 1, 256:384], r[:, 2:3], e[:, 0, 256:384],
                                       ALU.mult, ALU.add).then_inc(probs, 1)

            def k_evac(n, k):
                dve.wait_ge(piece_used, n + 1)
                V.tensor_copy(kT[:, 2 * k:2 * k + 2, :], ps[:, 1, :].rearrange("p (h t) -> p h t", h=2)).then_inc(k_out, 1)

            def v_evac(n, part):
                dve.wait_ge(piece_used, n + 1)
                V.tensor_copy(v[:, 1, 512 * part:512 * part + 512], ps[:, 1, :]).then_inc(v_out_d, 1)

            def head_norm(k):
                dve.wait_ge(o_out, 4 * k + 4)
                o = hn[:, :, 512 * k:512 * k + 512].rearrange("p b (h e) -> p b h e", h=4)

                def st(i):
                    return oss[:, i, 8 * k:8 * k + 8]
                link(V.tensor_tensor(o_sq, o, o, ALU.mult))
                link(V.tensor_reduce(st(2).rearrange("p (b h) -> p b h", b=NB), o_sq, axis=AX_X, op=ALU.add))
                V.tensor_scalar(st(0), st(2), 1.0 / VD, 1e-5, ALU.mult, ALU.add).then_inc(ovar, 1)
                dve.wait_ge(oroot, k + 1)
                rsqrt(st(2), st(0), st(1), st(3))
                for b in range(NB):
                    link(V.tensor_tensor(o[:, b], o[:, b],
                                         st(2)[:, 4 * b:4 * b + 4].unsqueeze(2).to_broadcast([P, 4, VD]), ALU.mult))
                for b in range(NB):
                    ins = V.tensor_tensor(o[:, b], o[:, b], subln_b.unsqueeze(1).to_broadcast([P, 4, VD]), ALU.mult)
                ins.then_inc(on_ready, 1)

            def add_to_x(banks):
                for k, bank in enumerate(banks):
                    b, half = divmod(k, 2)
                    xs = xres[:, b, 512 * half:512 * half + 512]
                    ins = V.tensor_tensor(xs, xs, ps[:, bank, :], ALU.add)
                    if half == 1:
                        ins.then_inc(x_ready, 1)

            norm(0)
            lo_upto(0)
            xt_split(0, range(4), 0)
            lo_upto(1)
            dve.wait_ge(rel_ps, 1)
            link(V.tensor_scalar(relT, ps[0:HEADS, 6, 0:BUCKETS], 1.0 / SCALE, None, ALU.mult))
            buckets = [bucket_of(n, BUCKETS, BUCKETS // 2, 128) for n in range(S)]
            V.memset(rel_row[:, S:3 * P], NEG / SCALE)
            for k in range(BUCKETS):
                n0, n1 = buckets.index(k), S - buckets[::-1].index(k)
                ins = V.tensor_copy(rel_row[:, S - n1:S - n0], relT[:, k:k + 1].to_broadcast([HEADS, n1 - n0]))
            ins.then_inc(rel_row_ok, 1)
            lo_upto(2)
            k_evac(1, 0)
            lo_upto(3)
            dve.wait_ge(in_small, 16 * 14)
            for k in range(2):
                V.tensor_tensor_reduce(out=lamj, in0=lamv[:, 2 * k, :], in1=lamv[:, 2 * k + 1, :], scale=1.0, scalar=0.0,
                                       op0=ALU.mult, op1=ALU.add, accum_out=lam_e[:, k:k + 1]).then_inc(lam_dot, 1)
                dve.wait_ge(lam_dot, k + 1)
            V.tensor_scalar(subln_b, subln_b, 1.0 - LAM_INIT, None, ALU.mult).then_inc(dve_link, 1)
            links[0] += 1
            dve.wait_ge(prm_ps, 1)
            V.tensor_copy(prm, ps[:, 7, 0:8 * RB]).then_inc(prm_ok, 1)
            lo_upto(4)
            dve.wait_ge(flip_ps, 1)
            V.tensor_copy(bias, ps[:, 4:8, :].rearrange("p a (h t) -> p (a h) t", h=2)).then_inc(bias_ok, 1)
            v_evac(3, 0)
            lo_upto(5)
            mask(0)
            lo_upto(6)
            dve.wait_ge(lam_exp, 1)
            link(V.scalar_tensor_tensor(neg_lam, lam_e[:, 1:2], -LAM_INIT, lam_e[:, 0:1], ALU.add, ALU.subtract))
            mix(0)
            mask(1)
            lo_upto(7)
            mix(1)
            k_evac(5, 1)
            mask(2)
            lo_upto(8)
            mix(2)
            mask(3)
            lo_upto(9)
            mix(3)
            k_evac(7, 2)
            mask(4)
            lo_upto(10)
            mix(4)
            mask(5)
            lo_upto(11)
            v_evac(9, 1)
            mix(5)
            head_norm(0)
            k_evac(11, 3)
            lo_upto(12)
            mask(6)
            xt_split(4, (6, 7), 0)
            mask(7)
            mix(6)
            lo_upto(13)
            mix(7)
            lo_upto(15)
            head_norm(1)
            xt_split(6, (2, 3), 4)
            lo_upto(16)
            dve.wait_ge(prm_ok, 1)
            link(V.tensor_scalar(lt[:, 0, :], lamp, -1.0, None, ALU.mult))
            V.tensor_tensor(lt[:, 0, :], lt[:, 0, :], lamp, ALU.max).then_inc(dl_ok, 1)
            dve.wait_ge(de_ok, 1)
            link(V.tensor_scalar(lt[:, 2, :], lt[:, 1, :], 2.0, None, ALU.add))
            link(V.reciprocal(lt[:, 2, :], lt[:, 2, :]))
            link(V.tensor_tensor(lt[:, 1, :], lt[:, 1, :], lt[:, 2, :], ALU.mult))
            link(V.tensor_tensor(lt[:, 2, :], lt[:, 1, :], lt[:, 1, :], ALU.mult))
            link(V.tensor_scalar(lt[:, 3, :], lt[:, 2, :], 1.0 / 17, None, ALU.mult))
            for k in range(15, 1, -2):
                link(V.scalar_tensor_tensor(lt[:, 3, :], lt[:, 3, :], 1.0 / k, lt[:, 2, :], ALU.add, ALU.mult))
            link(V.scalar_tensor_tensor(lt[:, 3, :], lt[:, 3, :], 1.0, lt[:, 1, :], ALU.add, ALU.mult))
            link(V.tensor_scalar(lt[:, 4, :], lamp, -1.0, 0.0, ALU.mult, ALU.max))
            link(V.scalar_tensor_tensor(lt[:, 4, :], lt[:, 3, :], 2.0, lt[:, 4, :], ALU.mult, ALU.add))
            V.tensor_scalar(decay, lt[:, 4, :], -4.0, None, ALU.mult).then_inc(decay_in, 1)
            V.tensor_scalar(decay2, lt[:, 4, :], -8.0, None, ALU.mult).then_inc(decay_in, 1)
            lo_upto(P_FFN + 2)
            dve.wait_ge(piece_used, P_FFN)
            add_to_x((6, 7, 0, 1))
            norm(1)
            xt_split(8, range(4), 0)

            def aT_split_lo(k, subs):
                dve.wait_ge(fh, k + 1)
                b = k % 2
                V.tensor_tensor(aT_lo[:, 0:subs, P * b:P * b + P],
                                ps[:, 2 + b, 0:P * subs].rearrange("p (s t) -> p s t", s=subs),
                                aT_hi[:, 0:subs, P * b:P * b + P].bitcast(F32), ALU.subtract).then_inc(fl, 1)

            for i in range(FC + 1):
                last = i == FC
                lo_upto(f_gate_at(i) + 2)
                if i:
                    aT_split_lo(2 * i - 2, 4)
                    aT_split_lo(2 * i - 1, 4)
                up_end = f_up_at(i) + (1 if last else 2)
                lo_upto(up_end + 1)
                dve.wait_ge(piece_used, up_end)
                for b in range(NB):
                    cols = 256 if last else CW
                    dve.wait_ge(fs, 2 * i + b + 1)
                    V.tensor_tensor(act_f[:, b, 0:cols], act_f[:, b, 0:cols], ps[:, 2 + b, 0:cols],
                                    ALU.mult).then_inc(fa, 1)
            aT_split_lo(2 * FC, 2)
            aT_split_lo(2 * FC + 1, 2)
            lo_upto(P_IN + 2)
            dve.wait_ge(piece_used, P_IN)
            add_to_x((4, 5, 6, 7))

            norm(2)
            V.memset(xb[:, :, 0:3], 0.0).then_inc(xb_zero, 1)
            xt_split(12, range(4), 0)

            def times(j):
                dve.wait_ge(ri_ok, 2 * j + 2)
                V.tensor_tensor(ix[:, 2 * j:2 * j + 2, :], ig, xc[:, j % 2], ALU.mult).then_inc(ix_ok, 1)

            for j in range(RB // 2):
                lo_upto(P_IN + j + 2)
                dve.wait_ge(xb_ok, j + 1)
                if j >= 2:
                    dve.wait_ge(ri_ps, j - 1)
                    dve.wait_ge(ix_ok, j - 1)
                for m in range(2):
                    b = 2 * j + m
                    V.tensor_scalar(xc[:, j % 2, m, :], xb[:, m, 3:3 + S], cvw[:, 3, b:b + 1], cvb[:, b:b + 1],
                                    ALU.mult, ALU.add).then_inc(dve_link, 1)
                links[0] += 2
                dve.wait_ge(dve_link, links[0])
                for tap in range(3):
                    for m in range(2):
                        b = 2 * j + m
                        ins = V.scalar_tensor_tensor(xc[:, j % 2, m, :], xb[:, m, tap:tap + S], cvw[:, tap, b:b + 1],
                                                     xc[:, j % 2, m, :], ALU.mult, ALU.add)
                        if (tap, m) == (2, 1):
                            ins.then_inc(xc_ok, 1)
                        else:
                            ins.then_inc(dve_link, 1)
                            links[0] += 1
                    if tap < 2:
                        dve.wait_ge(dve_link, links[0])
                if j:
                    times(j - 1)
            lo_upto(P_IN + RB // 2 + 2)
            dve.wait_ge(xc_ok, RB // 2)
            times(RB // 2 - 1)
            lo_upto(P_IN + RB // 2 + 3)
            dve.wait_ge(a_ok, RB)
            for g in range(2):
                n0, n1 = g * RB // 2, (g + 1) * RB // 2
                dve.wait_ge(sqt_ok, g + 1)
                link(V.scalar_tensor_tensor(hs[:, n0:n1, :], ra[:, n0:n1, :], 1.0, hs[:, n0:n1, :], ALU.add, ALU.mult))
                link(V.tensor_tensor(ix[:, n0:n1, :], ix[:, n0:n1, :], hs[:, n0:n1, :], ALU.mult))
                for n in range(n0, n1):
                    V.tensor_tensor_scan(hs[:, n, :], ra[:, n, :], ix[:, n, :], 0.0, ALU.mult,
                                         ALU.add).then_inc(dve_link, 1)
                    links[0] += 1
                lo_upto(P_IN + RB // 2 + 4 + g)
            dve.wait_ge(dve_link, links[0])
            for j in range(RB // 2):
                pair = gate[:, 2 * j:2 * j + 2, :]
                dve.wait_ge(gelu_ok, j + 1)
                V.tensor_tensor(pair, pair, hs[:, 2 * j:2 * j + 2, :], ALU.mult).then_inc(y_ok, 1)
                dve.wait_ge(yh_ok, j + 1)
                V.tensor_tensor(yT_lo[:, 2 * j:2 * j + 2, :], pair, yT_hi[:, 2 * j:2 * j + 2, :].bitcast(F32),
                                ALU.subtract).then_inc(yl_ok, 1)
                lo_upto(P_OUT + j + 2)
            lo_upto(P_MOE - 1)
            dve.wait_ge(piece_used, P_MOE)
            add_to_x((2, 3, 4, 5))

            norm(3)
            dve.wait_ge(late_consts, 4)
            V.memset(onehotT.bitcast(F32), 0.0).then_inc(oht_ok, 1)
            V.memset(combs[:, :, 0:1], 0.0)
            V.memset(slots[:, :, E + XP:E + XP + 1], -1.0)
            V.memset(rt_b[9], 1.0)
            for j in range(1, 4, 2):
                dve.wait_ge(xt_ps, 16 + j + 1)
                V.tensor_copy(xtf[:, 2 * j:2 * j + 2, :], ps[:, j, :].rearrange("p (c t) -> p c t", c=2)).then_inc(xtf_d, 1)
            for b in range(NB):
                dve.wait_ge(h_hi_ok, b + 1)
                V.tensor_tensor(h_lo[:, b, :], hn[:, b, :], h_hi[:, b, :].bitcast(F32), ALU.subtract).then_inc(h_lo_ok, 1)

            def bc(a):
                return a.to_broadcast([P, NB, E])

            def over_blocks(a):
                return a.unsqueeze(1).to_broadcast([P, NB, E])

            lg, eq, oh1, oh2, comb, sel, tmp = rt_b[0], rt_b[1], rt_b[2], rt_b[3], rt_b[4], rt_b[5], rt_b[6]
            m1, m2, mi = rt_b[7][:, :, 0:1], rt_b[7][:, :, 1:2], rt_b[7][:, :, 2:3]
            diff, e2, g1, g2 = (rt_b[8][:, :, k:k + 1] for k in range(4))
            order = rt_b[10][:, 0, :]
            dve.wait_ge(log_ps, 1)
            V.tensor_scalar(order, iota_e, -1.0, float(E), ALU.mult, ALU.add)
            link(V.tensor_copy(lg, ps[:, M0, 0:NB * E].rearrange("p (b e) -> p b e", b=NB)))

            def top(src, m, oh):
                link(V.tensor_reduce(m, src, axis=AX_X, op=ALU.max))
                link(V.tensor_tensor(eq, src, bc(m), ALU.is_equal))
                link(V.tensor_tensor(eq, eq, over_blocks(order), ALU.mult))
                link(V.tensor_reduce(mi, eq, axis=AX_X, op=ALU.max))
                link(V.tensor_tensor(oh, eq, bc(mi), ALU.is_equal))

            top(lg, m1, oh1)
            link(V.scalar_tensor_tensor(lg, oh1, -3e38, lg, ALU.mult, ALU.add))
            top(lg, m2, oh2)
            V.tensor_tensor(diff, m2, m1, ALU.subtract).then_inc(gexp_in, 1)
            link(V.tensor_tensor(sel, oh1, oh2, ALU.add))
            V.tensor_copy(sel16[:, :, :], sel).then_inc(sel_ok, 1)
            dve.wait_ge(pos_ps, 1)
            link(V.scalar_tensor_tensor(tmp, ps[:, M1, 0:NB * E].rearrange("p (b e) -> p b e", b=NB), 1.0, sel,
                                        ALU.add, ALU.mult))
            link(V.tensor_scalar(slots[:, :, 0:E], tmp, -1.0, None, ALU.add))

            def build_onehot(col, step):
                step(V.tensor_copy(g_cur.unsqueeze(2), col))
                for b in range(NB):
                    V.tensor_scalar(onehot[:, b, :], iota_s[:, :], g_cur[:, b:b + 1], None,
                                    ALU.is_equal).then_inc(oh_ok, 1)

            link(V.tensor_scalar(counts, ps[:, M1, NB * E:(NB + 1) * E], float(P), None, ALU.is_gt))
            build_onehot(slots[:, :, 0:1], link)
            lo_upto(P_MOE + 1)

            for j, b in enumerate((SB_, GB)):
                dve.wait_ge(gat_ps, 2 + j + 1)
                V.tensor_copy(xt_lo[:, 4 * j:4 * j + 4, 0:P],
                              ps[:, b, :].rearrange("p (c t) -> p c t", c=4)).then_inc(gat_lo, 1)

            lo_upto(P_MOE + HR - 1)

            def gate_weights():
                dve.wait_ge(gexp_ok, 1)
                link(V.tensor_scalar(g1, e2, 1.0, None, ALU.add))
                link(V.reciprocal(g1, g1))
                link(V.tensor_tensor(g2, e2, g1, ALU.mult))
                link(V.tensor_tensor(oh1, oh1, bc(g1), ALU.mult))
                link(V.tensor_tensor(oh2, oh2, bc(g2), ALU.mult))
                link(V.tensor_tensor(comb, oh1, oh2, ALU.add))
                link(V.tensor_copy(combs[:, :, 1:1 + E], comb))
                link(V.tensor_tensor_scan(ranks, rt_b[9][:, 0, :], counts, 0.0, ALU.mult, ALU.add))
                link(V.tensor_scalar(passes.bitcast(I32), ranks[0:1, E - 1:E], float(E), None, ALU.add))

            def further_pass(k):
                link(V.scalar_tensor_tensor(pick, ranks, float(k + 1), counts, ALU.is_equal, ALU.mult))
                link(V.tensor_tensor(tmp, slots[:, :, 0:E], over_blocks(pick), ALU.mult))
                link(V.tensor_reduce(mi, tmp, axis=AX_X, op=ALU.add))
                link(V.tensor_scalar(slots[:, :, E + k:E + k + 1], mi, float(-P), None, ALU.add))
                link(V.tensor_tensor(tmp, comb, over_blocks(pick), ALU.mult))
                link(V.tensor_reduce(combs[:, :, E + k + 1:E + k + 2], tmp, axis=AX_X, op=ALU.add))
                link(V.tensor_tensor(pick, pick, iota_e, ALU.mult))
                link(V.tensor_reduce(m1[:, 0, :], pick, axis=AX_X, op=ALU.add))
                ins = V.tensor_copy(extra[:, k:k + 1].bitcast(I32), m1[0:1, 0, :])
                if k == XP - 1:
                    ins.then_inc(route_ok, 1)
                else:
                    link(ins)

            V.sem_inc(ea_ok, 1)
            V.sem_inc(el_ok, 1)

            def expert(p):
                def lo(j):
                    if isinstance(p, int) and j < HR:
                        return
                    n = P_MOE + j
                    dve.wait_ge(hi_ready, p * PASS + (n + 1))
                    V.tensor_tensor(w_lo[:, half_slot(n), :], land(n), w_hi[:, half_slot(n), :].bitcast(F32),
                                    ALU.subtract).then_inc(lo_ready, 1)

                def eT_split_lo(i):
                    dve.wait_ge(eh_ok, p * EC + (i + 1))
                    V.tensor_tensor(eT_lo[i % 2], ps[:, TB, :].rearrange("p (s t) -> p s t", s=4),
                                    eT_hi[i % 2].bitcast(F32), ALU.subtract).then_inc(el_ok, 1)

                def gated(i):
                    dve.wait_ge(piece_used, p * PASS + (P_MOE + at(i) + 4))
                    dve.wait_ge(es_ok, p * EC + (i + 2))
                    V.tensor_tensor(act_e, act_e, ps[:, UB, :], ALU.mult).then_inc(ea_ok, 1)

                lo(0)
                lo(1)
                dve.wait_ge(ys_hi, p + 1)
                V.tensor_tensor(y_lo, ps[:, D0:D0 + 2, :].rearrange("p a n -> p (a n)"), y_hi.bitcast(F32),
                                ALU.subtract).then_inc(ys_lo, 1)
                V.tensor_copy(c_cur.unsqueeze(2), combs[:, :, bass.ds(p, 1)]).then_inc(cur_ok, 1)
                lo(2)
                lo(3)
                dve.wait_ge(cur_ok, p * 2 + 1)
                for k, bank in enumerate((M0, M1, SB_, TB)):
                    b, half = divmod(k, 2)
                    xs = xres[:, b, 512 * half:512 * half + 512]
                    dve.wait_ge(sc_ps, p * 4 + (k + 1))
                    V.scalar_tensor_tensor(xs, ps[:, bank, :], c_cur[:, b:b + 1], xs, ALU.mult,
                                           ALU.add).then_inc(sc_ok, 1)
                lo(4)
                gated(0)
                for i in range(1, EC):
                    g0 = at(i)
                    for j in range(1, 6):
                        lo(g0 + j)
                    eT_split_lo(i - 1)
                    if i == 1:
                        dve.wait_ge(oht_ps, p + 1)
                        V.tensor_copy(onehotT, ps[:, SB_, 0:S]).then_inc(oht_ok, 1)
                    if isinstance(p, int):
                        if i == 1:
                            gate_weights()
                        elif i < XP + 2:
                            further_pass(i - 2)
                    if i == 3:
                        dve.wait_ge(oht_ps, p + 1)
                        V.tensor_copy(g_cur.unsqueeze(2), slots[:, :, bass.ds(p + 1, 1)]).then_inc(cur_ok, 1)
                        dve.wait_ge(cur_ok, p * 2 + 2)
                        for b in range(NB):
                            V.tensor_scalar(onehot[:, b, :], iota_s[:, :], g_cur[:, b:b + 1], None,
                                            ALU.is_equal).then_inc(oh_ok, 1)
                    lo(g0 + 6)
                    gated(i)
                lo(PASS - 1)
                for j, b in enumerate((SB_, GB)):
                    dve.wait_ge(gat_ps, p * 4 + (4 + 2 + j + 1))
                    V.tensor_copy(xt_lo[:, 4 * j:4 * j + 4, 0:P],
                                  ps[:, b, :].rearrange("p (c t) -> p c t", c=4)).then_inc(gat_lo, 1)
                eT_split_lo(EC - 1)

            expert(0)
            dve.wait_ge(route_ok, 1)
            total = V.value_load(passes.bitcast(I32), min_val=E, max_val=E + XP)
            with V.Fori(1, total) as p:
                expert(p)
            dve.wait_ge(ys_hi, total + 1)
            V.tensor_tensor(y_lo, ps[:, D0:D0 + 2, :].rearrange("p a n -> p (a n)"), y_hi.bitcast(F32),
                            ALU.subtract).then_inc(ys_lo, 1)
            V.tensor_copy(c_cur.unsqueeze(2), combs[:, :, bass.ds(total, 1)]).then_inc(cur_ok, 1)
            dve.wait_ge(cur_ok, total * 2 + 1)
            for k, bank in enumerate((M0, M1, SB_, TB)):
                b, half = divmod(k, 2)
                xs = xres[:, b, 512 * half:512 * half + 512]
                dve.wait_ge(sc_ps, total * 4 + (k + 1))
                V.scalar_tensor_tensor(xs, ps[:, bank, :], c_cur[:, b:b + 1], xs, ALU.mult, ALU.add).then_inc(sc_ok, 1)
            norm(4)

        @block.tensor
        def _(pe):
            T = nc.tensor

            def mm3(acc, xh, xl, wh, wl, start, stop, weights_stay=False):
                terms = ((xh, wh), (xl, wh), (xh, wl))
                for k, (a, b) in enumerate(terms):
                    stationary, moving = (b, a) if weights_stay else (a, b)
                    ins = T.matmul(acc, stationary, moving, start=start and k == 0, stop=stop and k == 2)
                return ins

            def piece(n):
                pe.wait_ge(lo_ready, n + 1)
                return w_hi[:, half_slot(n), :], w_lo[:, half_slot(n), :]

            def project8(n, bank, xt_from=None):
                wh, wl = (w.rearrange("p (c n) -> p c n", c=KC) for w in piece(n))
                for m in range(2):
                    for c in range(KC):
                        if xt_from is not None and m == 0 and c % 2 == 0:
                            pe.wait_ge(xt_lo_ok, xt_from + c // 2 + 1)
                        ins = mm3(ps[:, bank, 256 * m:256 * m + 256], xt_hi[:, c, :], xt_lo[:, c, :],
                                  wh[:, c, P * m:P * m + P], wl[:, c, P * m:P * m + P], c == 0, c == KC - 1, True)
                ins.then_inc(piece_used, 1)

            def project4(n, banks, half, c_of=0, close=None):
                wh, wl = (w.rearrange("p (c n) -> p c n", c=4) for w in piece(n))
                for c in range(4):
                    for b, bank in enumerate(banks):
                        t = slice(P * b, P * b + P)
                        ins = mm3(ps[:, bank, :], xt_hi[:, 4 * half + c, t], xt_lo[:, 4 * half + c, t],
                                  wh[:, c, :], wl[:, c, :], half == 0 and c == 0, half == 1 and c == 3)
                ins.then_inc(piece_used, 1)

            def down(n, banks, ah, al, subs, first, last):
                wh, wl = (w.rearrange("p (s n) -> p s n", s=2) for w in piece(n))
                for s, sub in enumerate(subs):
                    for k, bank in enumerate(banks):
                        b, half = divmod(k, 2)
                        t, o = slice(P * b, P * b + P), slice(512 * half, 512 * half + 512)
                        ins = mm3(ps[:, bank, :], ah[:, sub, t], al[:, sub, t], wh[:, s, o], wl[:, s, o],
                                  first and s == 0, last and s == 1)
                ins.then_inc(piece_used, 1)

            def transpose_hn(banks, c0, norm=None):
                for b in range(NB):
                    if norm is not None:
                        pe.wait_ge(hn_ready, 2 * norm + b + 1)
                    for j, bank in enumerate(banks):
                        for m in range(2):
                            c, o = c0 + 2 * j + m, 256 * m + P * b
                            ins = T.transpose(ps[:, bank, o:o + P], hn[:, b, P * c:P * c + P], ident[:, :])
                        if b == NB - 1:
                            ins.then_inc(xt_ps, 1)

            def keep_warm(bank, n):
                for _ in range(n):
                    T.matmul(ps[:, bank, :], xt_hi[:, 0, 0:P], xt_hi[:, 0:2, :], start=True, stop=True)

            def scores(h):
                if h:
                    pe.wait_ge(masked, 4 * h)
                pe.wait_ge(q_out, h // 2 + 1)
                pe.wait_ge(k_out, h // 2 + 1)
                for c in range(2):
                    rows = slice(HD * c, HD * c + HD)
                    T.matmul(ps[:, 4 + c, 0:256], qT[rows, h, P:S], kT[rows, h, 0:S], start=True, stop=True)
                    ins = T.matmul(ps[:, 4 + c, 256:384], qT[rows, h, 0:P], kT[rows, h, 0:P], start=True, stop=True)
                ins.then_inc(s_done, 1)

            def turn(h):
                pe.wait_ge(probs, h + 1)
                if h:
                    pe.wait_ge(aT_ok, h)
                for k in range(3):
                    ins = T.transpose(ps[:, 2, P * k:P * k + P], ex[:, h % 2, 0, P * k:P * k + P], ident[:, :])
                ins.then_inc(t_done, 1)

            def values(h):
                pe.wait_ge(aT_ok, h + 1)
                pe.wait_ge(v_out_a, h // 4 + 1)
                pe.wait_ge(v_out_d, h // 4 + 1)
                if h:
                    pe.wait_ge(o_out, h)
                e = slice(VD * h, VD * h + VD)
                a = aT[:, h % 2, :]
                T.matmul(ps[:, 3, 0:P], a[:, 256:384], v[:, 0, e], start=True, stop=True)
                T.matmul(ps[:, 3, P:2 * P], a[:, 0:128], v[:, 0, e], start=True, stop=False)
                T.matmul(ps[:, 3, P:2 * P], a[:, 128:256], v[:, 1, e], start=False, stop=True).then_inc(o_done, 1)

            pe.wait_ge(consts, 2)
            transpose_hn(range(4), 0, norm=0)
            pe.wait_ge(in_table, 16)
            T.transpose(ps[0:HEADS, 6, 0:BUCKETS], rel_in[0:BUCKETS, :], ident[0:BUCKETS, 0:BUCKETS]).then_inc(rel_ps, 1)
            pe.wait_ge(xt_lo_ok, 1)
            project8(0, 0, xt_from=0)
            project8(1, 1)
            pe.wait_ge(in_small, 16 * 14)
            T.transpose(ps[:, 7, 0:8 * RB], rows_in[0:8 * RB, :], ident[0:8 * RB, 0:8 * RB]).then_inc(prm_ps, 1)
            pe.wait_ge(q_out, 1)
            pe.wait_ge(k_out, 1)
            project4(2, (0, 1), 0)
            pe.wait_ge(in_rel, 16)
            pe.wait_ge(prm_ok, 1)
            for k in range(4):
                ins = T.matmul(ps[:, 4 + k, :], flip, bias_up[:, 512 * k:512 * k + 512], start=True, stop=True)
            ins.then_inc(flip_ps, 1)
            project4(3, (0, 1), 1)
            pe.wait_ge(bias_ok, 1)
            scores(0)
            pe.wait_ge(v_out_a, 1)
            project8(4, 0)
            scores(1)
            turn(0)
            pe.wait_ge(v_out_d, 1)
            project8(5, 1)
            values(0)
            scores(2)
            turn(1)
            project8(6, 0)
            values(1)
            scores(3)
            turn(2)
            pe.wait_ge(k_out, 2)
            project8(7, 1)
            values(2)
            scores(4)
            turn(3)
            project4(8, (0, 1), 0)
            values(3)
            scores(5)
            turn(4)
            project4(9, (0, 1), 1)
            pe.wait_ge(v_out_a, 2)
            pe.wait_ge(v_out_d, 2)
            project8(10, 0)
            values(4)
            turn(5)
            project8(11, 1)
            values(5)
            scores(6)
            pe.wait_ge(on_ready, 1)
            transpose_hn((6, 7), 0)
            scores(7)
            pe.wait_ge(xt_lo_ok, 6)

            def attn_out(n, half, g):
                project4(n, ((6, 0), (7, 1))[g], half)

            attn_out(P_WO, 0, 0)
            turn(6)
            values(6)
            turn(7)
            values(7)
            attn_out(P_WO + 1, 0, 1)
            pe.wait_ge(on_ready, 2)
            pe.wait_ge(aT_ok, 8)
            pe.wait_ge(o_out, 8)
            transpose_hn((2, 3), 4)
            pe.wait_ge(xt_lo_ok, 8)
            attn_out(P_WO + 2, 1, 0)
            attn_out(P_WO + 3, 1, 1)

            keep_warm(2, 24)
            transpose_hn(range(4), 0, norm=1)
            pe.wait_ge(xt_lo_ok, 10)

            def turn_chunk(i, subs):
                for b in range(NB):
                    pe.wait_ge(fa, 2 * i + b + 1)
                    for s in range(subs):
                        ins = T.transpose(ps[:, 2 + b, P * s:P * s + P], act_f[:, b, P * s:P * s + P], ident[:, :])
                    ins.then_inc(ft, 1)

            def narrow(n, banks):
                wh, wl = (w.rearrange("p (c n) -> p c n", c=KC) for w in piece(n))
                for c in range(KC):
                    for b, bank in enumerate(banks):
                        t = slice(P * b, P * b + P)
                        ins = mm3(ps[:, bank, 0:256], xt_hi[:, c, t], xt_lo[:, c, t], wh[:, c, :], wl[:, c, :],
                                  c == 0, c == KC - 1)
                ins.then_inc(piece_used, 1)

            for i in range(FC + 1):
                last = i == FC
                if i:
                    pe.wait_ge(fs, 2 * i)
                if last:
                    narrow(f_gate_at(i), (0, 1))
                    turn_chunk(i - 1, 4)
                else:
                    project4(f_gate_at(i), (0, 1), 0)
                    if i == 0:
                        pe.wait_ge(xt_lo_ok, 12)
                    if i:
                        turn_chunk(i - 1, 4)
                    project4(f_gate_at(i) + 1, (0, 1), 1)
                if i:
                    pe.wait_ge(fl, 2 * i)
                    for h in range(2):
                        down(f_down_at(i - 1) + h, (4, 5, 6, 7), aT_hi, aT_lo, (2 * h, 2 * h + 1), i == 1 and h == 0, False)
                if last:
                    narrow(f_up_at(i), (2, 3))
                else:
                    project4(f_up_at(i), (2, 3), 0)
                    project4(f_up_at(i) + 1, (2, 3), 1)
            turn_chunk(FC, 2)
            pe.wait_ge(fl, 2 * FC + 2)
            down(f_down_at(FC), (4, 5, 6, 7), aT_hi, aT_lo, (0, 1), False, True)

            keep_warm(0, 24)
            transpose_hn(range(4), 0, norm=2)
            pe.wait_ge(in_lru, 32)

            def gates(j):
                pe.wait_ge(xc_ok, j + 1)
                if j:
                    pe.wait_ge(t_ok, 2 * j)
                for m in range(2):
                    for w, bank in ((wga, 2), (wgx, 3)):
                        ins = T.matmul(ps[:, bank, 256 * m:256 * m + 256], w[:, 2 * j + m, :], xc[:, j % 2, m, :],
                                       start=True, stop=True)
                ins.then_inc(ri_ps, 1)

            for j in range(RB // 2):
                if j >= 2:
                    pe.wait_ge(xb_ok, j - 1)
                project8(P_IN + j, j % 2, xt_from=None if j else 12)
                if j:
                    gates(j - 1)
            for j, bank in enumerate(GATE_BANKS):
                if j in (2, 3):
                    pe.wait_ge(xb_ok, j + 2)
                if j == 4:
                    pe.wait_ge(gelu_ok, 1)
                project8(P_IN + RB // 2 + j, bank)
                if j == 0:
                    gates(RB // 2 - 1)
            pe.wait_ge(t_ok, RB)
            for j in range(RB // 2):
                pe.wait_ge(yl_ok, j + 1)
                down(P_OUT + j, (2, 3, 4, 5), yT_hi, yT_lo, (2 * j, 2 * j + 1), j == 0, j == RB // 2 - 1)

            keep_warm(0, 24)
            transpose_hn(range(4), 0, norm=3)
            pe.wait_ge(xtf_a, 2)
            pe.wait_ge(xtf_d, 2)
            for b in range(NB):
                for c in range(KC):
                    ins = T.matmul(ps[:, M0, E * b:E * b + E], xtf[:, c, P * b:P * b + P], rw[:, c, :],
                                   start=c == 0, stop=c == KC - 1)
            ins.then_inc(log_ps, 1)
            keep_warm(0, 20)
            pe.wait_ge(late_consts, 4)
            pe.wait_ge(sel_ok, 1)
            T.matmul(ps[:, M1, 0:E], tri[:, :], sel16[:, 0, :], start=True, stop=True)
            T.matmul(ps[:, M1, E:2 * E], ones[:, :], sel16[:, 0, :], start=True, stop=False)
            T.matmul(ps[:, M1, E:2 * E], tri[:, :], sel16[:, 1, :], start=False, stop=True)
            T.matmul(ps[:, M1, 2 * E:3 * E], ones[:, :], sel16[:, 0, :], start=True, stop=False)
            T.matmul(ps[:, M1, 2 * E:3 * E], ones[:, :], sel16[:, 1, :], start=False, stop=True).then_inc(pos_ps, 1)

            keep_warm(0, 12)

            def gather(parts):
                for k in parts:
                    h, bank, j = (h_hi, h_hi, h_lo, h_lo)[k], (M0, M1, SB_, GB)[k], k % 2
                    for m in range(4):
                        c = 4 * j + m
                        for b in range(NB):
                            ins = T.matmul(ps[:, bank, P * m:P * m + P], h[:, b, P * c:P * c + P], onehot[:, b, :],
                                           start=b == 0, stop=b == NB - 1)
                    ins.then_inc(gat_ps, 1)

            def scatter():
                for k, bank in enumerate((M0, M1, SB_, TB)):
                    b, half = divmod(k, 2)
                    o = slice(512 * half, 512 * half + 512)
                    T.matmul(ps[:, bank, :], onehotT[:, P * b:P * b + P], y_hi[:, o], start=True, stop=False)
                    T.matmul(ps[:, bank, :], onehotT[:, P * b:P * b + P], y_lo[:, o], start=False,
                             stop=True).then_inc(sc_ps, 1)

            pe.wait_ge(h_lo_ok, 2)
            pe.wait_ge(oh_ok, 2)
            gather(range(4))

            T.sem_inc(et_ps, 1)

            def expert(p):
                def slot(j):
                    n = P_MOE + j
                    pe.wait_ge(lo_ready, p * PASS + (n + 1))
                    return w_hi[:, half_slot(n), :], w_lo[:, half_slot(n), :]

                def up_or_gate(j, bank, half):
                    wh, wl = (w.rearrange("p (c n) -> p c n", c=4) for w in slot(j))
                    for c in range(4):
                        ins = mm3(ps[:, bank, :], xt_hi[:, 4 * half + c, 0:P], xt_lo[:, 4 * half + c, 0:P],
                                  wh[:, c, :], wl[:, c, :], half == 0 and c == 0, half == 1 and c == 3)
                    ins.then_inc(piece_used, 1)

                def down_e(j, i, h):
                    wh, wl = (w.rearrange("p (s n) -> p s n", s=2) for w in slot(j))
                    for s in range(2):
                        for half, bank in enumerate((D0, D1)):
                            o = slice(512 * half, 512 * half + 512)
                            ins = mm3(ps[:, bank, :], eT_hi[i % 2][:, 2 * h + s, :], eT_lo[i % 2][:, 2 * h + s, :],
                                      wh[:, s, o], wl[:, s, o], (i, h, s) == (0, 0, 0), (i, h, s) == (EC - 1, 1, 1))
                    ins.then_inc(piece_used, 1)

                def turn_e(i):
                    pe.wait_ge(ea_ok, p * EC + (i + 2))
                    pe.wait_ge(el_ok, p * EC + (i + 1))
                    for s in range(4):
                        ins = T.transpose(ps[:, TB, P * s:P * s + P], act_e[:, P * s:P * s + P], ident[:, :])
                    ins.then_inc(et_ps, 1)

                for i in range(EC):
                    g0 = at(i)
                    pe.wait_ge(es_ok, p * EC + (i + 1))
                    if i == 0:
                        pe.wait_ge(gat_hi, p * 2 + 2)
                        pe.wait_ge(gat_lo, p * 2 + 2)
                    up_or_gate(g0, GB, 0)
                    up_or_gate(g0 + 1, GB, 1)
                    if i == 0:
                        pe.wait_ge(ys_lo, p + 1)
                        pe.wait_ge(oht_ok, p + 1)
                        pe.wait_ge(el_ok, p * EC + 1)
                        scatter()
                    else:
                        if i == 1:
                            pe.wait_ge(sc_ok, p * 4 + 4)
                            pe.wait_ge(oh_ok, p * 2 + 2)
                        turn_e(i - 1)
                        if i == 1:
                            for b in range(NB):
                                ins = T.transpose(ps[:, SB_, P * b:P * b + P], onehot[:, b, :].bitcast(F32), ident[:, :])
                            ins.then_inc(oht_ps, 1)
                    pe.wait_ge(ea_ok, p * EC + (i + 1))
                    up_or_gate(g0 + 2, UB, 0)
                    up_or_gate(g0 + 3, UB, 1)
                    if i == EC - 1:
                        pe.wait_ge(oh_ok, p * 2 + 4)
                        pe.wait_ge(oht_ok, p + 2)
                        pe.wait_ge(es_ok, p * EC + (EC + 1))
                        gather(range(4))
                    if i:
                        pe.wait_ge(el_ok, p * EC + (i + 1))
                        down_e(g0 + 4, i - 1, 0)
                        if i == EC - 1:
                            turn_e(i)
                        down_e(g0 + 5, i - 1, 1)
                pe.wait_ge(el_ok, p * EC + (EC + 1))
                down_e(PASS - 2, EC - 1, 0)
                down_e(PASS - 1, EC - 1, 1)

            expert(0)
            pe.wait_ge(route_ok, 1)
            total = T.value_load(passes.bitcast(I32), min_val=E, max_val=E + XP)
            with T.Fori(1, total) as p:
                expert(p)
            pe.wait_ge(ys_lo, total + 1)
            pe.wait_ge(oht_ok, total + 1)
            pe.wait_ge(gat_hi, total * 2 + 2)
            pe.wait_ge(gat_lo, total * 2 + 2)
            pe.wait_ge(el_ok, total * EC + 1)
            scatter()


_INS = ["x", "norm_mix", "norm_ffn", "norm_final", "rel_bias", "attn_w_qkv", "attn_w_o", "attn_lambda_q1",
        "attn_lambda_k1", "attn_lambda_q2", "attn_lambda_k2", "attn_subln", "lru_w_in", "lru_conv_w", "lru_conv_b",
        "lru_gate_a_w", "lru_gate_a_b", "lru_gate_x_w", "lru_gate_x_b", "lru_lambda", "lru_w_out", "ffn_w_gate",
        "ffn_w_up", "ffn_w_down", "moe_router", "moe_w_gate", "moe_w_up", "moe_w_down"]


def kernel(**inputs):
    import numpy as _np
    import concourse.bacc as _bacc
    from concourse import mybir as _mybir
    from concourse.bass_utils import run_bass_kernel_spmd as _run

    nc = _bacc.Bacc("TRN2", target_bir_lowering=False, num_devices=1)
    arrays, args = {}, []
    for name in _INS:
        a = _np.ascontiguousarray(inputs[name])
        arrays[f"in_{name}_dram"] = a
        args.append(nc.dram_tensor(f"in_{name}_dram", a.shape, _mybir.dt.from_np(a.dtype), kind="ExternalInput").ap())
    out = nc.dram_tensor("out_0_dram", inputs["x"].shape, _mybir.dt.float32, kind="ExternalOutput").ap()
    build_trunk(nc, *args, out)
    r = _run(nc, [arrays], core_ids=[0])
    return r.results[0]["out_0_dram"]
```
